# Optimizing a Trainium2 kernel written in Bass

```python
import math
import jax, jax.numpy as jnp
from jax import lax
import numpy as np

D_MODEL = 1024
BATCH = 1
SEQ = 1024
DEPTH = 1
DEC_BATCH = 1
DEC_SEQ = 32
PAST_LEN = 512

CHUNK = 64
N_HEADS = 16
N_KV_HEADS = 4
HEAD_DIM = 64
GROUP = N_HEADS // N_KV_HEADS
ROT_DIM = HEAD_DIM // 4
ROPE_THETA = 500000.0
WINDOW = 128
WIN_CHUNKS = WINDOW // CHUNK
ATTN_SCALE = HEAD_DIM ** -0.5
LRU_WIDTH = D_MODEL
LRU_BLOCKS = 16
LRU_BLOCK_DIM = LRU_WIDTH // LRU_BLOCKS
LRU_C = 8.0
CONV_W = 4
D_FF = -(-8 * D_MODEL // (3 * 256)) * 256
Q_W = N_HEADS * HEAD_DIM
KV_W = N_KV_HEADS * HEAD_DIM
N_IN = Q_W + 2 * KV_W + 2 * LRU_WIDTH + 2 * D_MODEL
IN_SPLITS = (Q_W, Q_W + KV_W, Q_W + 2 * KV_W, Q_W + 2 * KV_W + LRU_WIDTH, Q_W + 2 * KV_W + 2 * LRU_WIDTH)
RMS_EPS = 1e-6
NEG_INF = -1e30

kernel_name = "hybrid_swa_sink_rglru_streaming_step"

def rms_norm(x, g):
    x32 = x.astype(jnp.float32)
    y = x32 * lax.rsqrt(jnp.mean(x32 * x32, axis=-1, keepdims=True) + RMS_EPS)
    return (y * g.astype(jnp.float32)).astype(x.dtype)

def partial_rope(x, positions):
    freqs = ROPE_THETA ** (-jnp.arange(0, ROT_DIM, 2, dtype=jnp.float32) / ROT_DIM)
    ang = positions.astype(jnp.float32)[:, None] * freqs[None, :]
    cos = jnp.cos(ang)[None, :, None, :]
    sin = jnp.sin(ang)[None, :, None, :]
    xr = x[..., :ROT_DIM].astype(jnp.float32)
    x1, x2 = xr[..., : ROT_DIM // 2], xr[..., ROT_DIM // 2:]
    rot = jnp.concatenate([x1 * cos - x2 * sin, x2 * cos + x1 * sin], axis=-1)
    return jnp.concatenate([rot.astype(x.dtype), x[..., ROT_DIM:]], axis=-1)

def sink_attend(q, k, v, mask, sinks):
    s = jnp.einsum('bnqkgd,bnskd->bnkgqs', q, k).astype(jnp.float32) * ATTN_SCALE
    s = jnp.where(mask[None, :, None, None, :, :], s, NEG_INF)
    sink = sinks.astype(jnp.float32).reshape(N_KV_HEADS, GROUP)[:, :, None, None]
    m = jnp.maximum(jnp.max(s, axis=-1, keepdims=True), sink)
    p = jnp.exp(s - m)
    den = jnp.sum(p, axis=-1, keepdims=True) + jnp.exp(sink - m)
    p = (p / den).astype(v.dtype)
    return jnp.einsum('bnkgqs,bnskd->bnqkgd', p, v)

def shift_chunks(xb, j):
    if j == 0:
        return xb
    return jnp.concatenate([jnp.zeros_like(xb[:, :j]), xb[:, :-j]], axis=1)

def banded_window_attention(q, k, v, sinks):
    B, T = q.shape[:2]
    nc = T // CHUNK
    qb = q.reshape(B, nc, CHUNK, N_KV_HEADS, GROUP, HEAD_DIM)
    kb = k.reshape(B, nc, CHUNK, N_KV_HEADS, HEAD_DIM)
    vb = v.reshape(B, nc, CHUNK, N_KV_HEADS, HEAD_DIM)
    shifts = list(range(WIN_CHUNKS - 1, -1, -1))
    kk = jnp.concatenate([shift_chunks(kb, j) for j in shifts], axis=2)
    vv = jnp.concatenate([shift_chunks(vb, j) for j in shifts], axis=2)
    cidx = jnp.arange(nc)
    mask = jnp.concatenate(
        [jnp.broadcast_to((cidx >= j)[:, None, None], (nc, CHUNK, CHUNK)) for j in shifts], axis=-1)
    o = sink_attend(qb, kk, vv, mask, sinks)
    return o.reshape(B, T, N_HEADS, HEAD_DIM)

def cached_window_attention(q, k, v, k_cache, v_cache, sinks, positions):
    B, T = q.shape[:2]
    kk = jnp.concatenate([k_cache.astype(k.dtype), k], axis=1)
    vv = jnp.concatenate([v_cache.astype(v.dtype), v], axis=1)
    kpos = PAST_LEN - WINDOW + jnp.arange(WINDOW + T)
    qc = positions // CHUNK
    kc = kpos // CHUNK
    mask = (kc[None, :] > qc[:, None] - WIN_CHUNKS) & (kc[None, :] <= qc[:, None])
    o = sink_attend(q.reshape(B, 1, T, N_KV_HEADS, GROUP, HEAD_DIM), kk[:, None], vv[:, None], mask[None], sinks)
    return o.reshape(B, T, N_HEADS, HEAD_DIM), kk[:, -WINDOW:], vv[:, -WINDOW:]

def lin_combine(left, right):
    a1, b1 = left
    a2, b2 = right
    return a1 * a2, a2 * b1 + b2

def rg_lru(xc, h0, w_rg, b_rg, w_ig, b_ig, lru_lambda, stream_start):
    B, T, _ = xc.shape
    xb = xc.reshape(B, T, LRU_BLOCKS, LRU_BLOCK_DIM)
    r = jax.nn.sigmoid((jnp.einsum('btnd,nde->btne', xb, w_rg).reshape(B, T, LRU_WIDTH) + b_rg).astype(jnp.float32))
    i = jax.nn.sigmoid((jnp.einsum('btnd,nde->btne', xb, w_ig).reshape(B, T, LRU_WIDTH) + b_ig).astype(jnp.float32))
    log_a = -LRU_C * r * jax.nn.softplus(-lru_lambda.astype(jnp.float32))
    a = jnp.exp(log_a)
    mult = jnp.sqrt(-jnp.expm1(2.0 * log_a))
    if stream_start:
        mult = mult.at[:, 0].set(1.0)
    b = mult * i * xc.astype(jnp.float32)
    b = b.at[:, 0].add(a[:, 0] * h0.astype(jnp.float32))
    _, h = lax.associative_scan(lin_combine, (a, b), axis=1)
    return h.astype(xc.dtype), h[:, -1].astype(xc.dtype)

def trunk_layer(x, positions, k_cache, v_cache, conv_state, h0, stream_start,
                attn_norm, w_in, q_norm, k_norm, sinks, conv_w, conv_b, w_rg, b_rg, w_ig, b_ig,
                lru_lambda, w_attn_out, w_lru_out, w_o, ffn_norm, w_gate_up, w_down):
    B, T, _ = x.shape
    xn = rms_norm(x, attn_norm)
    z = xn @ w_in
    q, k, v, xl, yg, gl = jnp.split(z, IN_SPLITS, axis=-1)
    q = partial_rope(rms_norm(q.reshape(B, T, N_HEADS, HEAD_DIM), q_norm), positions)
    k = partial_rope(rms_norm(k.reshape(B, T, N_KV_HEADS, HEAD_DIM), k_norm), positions)
    v = v.reshape(B, T, N_KV_HEADS, HEAD_DIM)
    if k_cache is None:
        o = banded_window_attention(q, k, v, sinks)
        k_buf, v_buf = k[:, -WINDOW:], v[:, -WINDOW:]
    else:
        o, k_buf, v_buf = cached_window_attention(q, k, v, k_cache, v_cache, sinks, positions)
    attn_branch = o.reshape(B, T, Q_W) @ w_attn_out
    xp = jnp.concatenate([conv_state.astype(xl.dtype), xl], axis=1)
    xc = conv_b + xp[:, 0:T] * conv_w[0]
    for j in range(1, CONV_W):
        xc = xc + xp[:, j:j + T] * conv_w[j]
    new_conv = xp[:, -(CONV_W - 1):]
    h, h_last = rg_lru(xc, h0, w_rg, b_rg, w_ig, b_ig, lru_lambda, stream_start)
    lru_branch = (h * jax.nn.gelu(yg)) @ w_lru_out
    g_a, g_b = jnp.split(jax.nn.sigmoid(gl), 2, axis=-1)
    x = x + (g_a * attn_branch + g_b * lru_branch) @ w_o
    gate, up = jnp.split(rms_norm(x, ffn_norm) @ w_gate_up, 2, axis=-1)
    x = x + (jax.nn.silu(gate) * up) @ w_down
    return x, k_buf, v_buf, new_conv, h_last

def setup_inputs(seed: int = 0) -> dict:
    key = jax.random.key(seed)
    ks = jax.random.split(key, 26)
    f32 = jnp.float32
    nrm = lambda k, shape, s: jax.random.normal(k, shape, f32) * s
    u = jax.random.uniform(ks[16], (DEPTH, LRU_WIDTH), f32, minval=0.9, maxval=0.999)
    base = u ** (1.0 / LRU_C)
    lru_lambda = jnp.log(base) - jnp.log1p(-base)
    return {
        "x_prompt": nrm(ks[0], (BATCH, SEQ, D_MODEL), 1.0),
        "x_sample": nrm(ks[1], (DEC_BATCH, DEC_SEQ, D_MODEL), 1.0),
        "cache_k": nrm(ks[2], (DEPTH, DEC_BATCH, WINDOW, N_KV_HEADS, HEAD_DIM), 1.0),
        "cache_v": nrm(ks[3], (DEPTH, DEC_BATCH, WINDOW, N_KV_HEADS, HEAD_DIM), 1.0),
        "state_conv": nrm(ks[4], (DEPTH, DEC_BATCH, CONV_W - 1, LRU_WIDTH), 1.0),
        "state_lru": nrm(ks[5], (DEPTH, DEC_BATCH, LRU_WIDTH), 0.5),
        "attn_norm": 1.0 + nrm(ks[6], (DEPTH, D_MODEL), 0.05),
        "w_in": nrm(ks[7], (DEPTH, D_MODEL, N_IN), D_MODEL ** -0.5),
        "q_norm": 1.0 + nrm(ks[8], (DEPTH, HEAD_DIM), 0.05),
        "k_norm": 1.0 + nrm(ks[9], (DEPTH, HEAD_DIM), 0.05),
        "sinks": nrm(ks[10], (DEPTH, N_HEADS), 0.5),
        "conv_w": nrm(ks[11], (DEPTH, CONV_W, LRU_WIDTH), CONV_W ** -0.5),
        "conv_b": nrm(ks[12], (DEPTH, LRU_WIDTH), 0.01),
        "w_rg": nrm(ks[13], (DEPTH, LRU_BLOCKS, LRU_BLOCK_DIM, LRU_BLOCK_DIM), LRU_BLOCK_DIM ** -0.5),
        "b_rg": nrm(ks[14], (DEPTH, LRU_WIDTH), 0.01),
        "w_ig": nrm(ks[15], (DEPTH, LRU_BLOCKS, LRU_BLOCK_DIM, LRU_BLOCK_DIM), LRU_BLOCK_DIM ** -0.5),
        "b_ig": nrm(ks[17], (DEPTH, LRU_WIDTH), 0.01),
        "lru_lambda": lru_lambda,
        "w_attn_out": nrm(ks[18], (DEPTH, Q_W, D_MODEL), Q_W ** -0.5),
        "w_lru_out": nrm(ks[19], (DEPTH, LRU_WIDTH, D_MODEL), LRU_WIDTH ** -0.5),
        "w_o": nrm(ks[20], (DEPTH, D_MODEL, D_MODEL), D_MODEL ** -0.5),
        "ffn_norm": 1.0 + nrm(ks[21], (DEPTH, D_MODEL), 0.05),
        "w_gate_up": nrm(ks[22], (DEPTH, D_MODEL, 2 * D_FF), D_MODEL ** -0.5),
        "w_down": nrm(ks[23], (DEPTH, D_FF, D_MODEL), D_FF ** -0.5),
    }

def reference(x_prompt, x_sample, cache_k, cache_v, state_conv, state_lru,
              attn_norm, w_in, q_norm, k_norm, sinks, conv_w, conv_b, w_rg, b_rg, w_ig, b_ig,
              lru_lambda, w_attn_out, w_lru_out, w_o, ffn_norm, w_gate_up, w_down):
    Bp, Tp, _ = x_prompt.shape
    Bs, Ts, _ = x_sample.shape
    pos_p = jnp.arange(Tp)
    pos_s = PAST_LEN + jnp.arange(Ts)
    conv0 = jnp.zeros((Bp, CONV_W - 1, LRU_WIDTH), x_prompt.dtype)
    h0 = jnp.zeros((Bp, LRU_WIDTH), x_prompt.dtype)
    xp, xs = x_prompt, x_sample
    kp_l, vp_l, cp_l, hp_l = [], [], [], []
    ks_l, vs_l, cs_l, hs_l = [], [], [], []
    for l in range(DEPTH):
        w = (attn_norm[l], w_in[l], q_norm[l], k_norm[l], sinks[l], conv_w[l], conv_b[l], w_rg[l], b_rg[l],
             w_ig[l], b_ig[l], lru_lambda[l], w_attn_out[l], w_lru_out[l], w_o[l], ffn_norm[l],
             w_gate_up[l], w_down[l])
        xp, kb, vb, cb, hb = trunk_layer(xp, pos_p, None, None, conv0, h0, True, *w)
        kp_l.append(kb); vp_l.append(vb); cp_l.append(cb); hp_l.append(hb)
        xs, kb, vb, cb, hb = trunk_layer(xs, pos_s, cache_k[l], cache_v[l], state_conv[l], state_lru[l], False, *w)
        ks_l.append(kb); vs_l.append(vb); cs_l.append(cb); hs_l.append(hb)
    return (xp, xs,
            jnp.stack(kp_l), jnp.stack(vp_l), jnp.stack(cp_l), jnp.stack(hp_l),
            jnp.stack(ks_l), jnp.stack(vs_l), jnp.stack(cs_l), jnp.stack(hs_l))


_drawn_inputs = setup_inputs


def setup_inputs(seed=0):
    import zlib

    import numpy as np

    out = dict(_drawn_inputs(seed))
    spreads = {}
    factors = {'q_norm': 8.0, 'sinks': 64.0, 'b_rg': 23.002, 'b_ig': 8.0}
    for name, (base, spread) in spreads.items():
        noise = np.random.default_rng([zlib.crc32(name.encode()), seed]).standard_normal(out[name].shape)
        drawn = base * np.exp(spread * noise) if base else spread * noise
        out[name] = __import__('jax').numpy.asarray(drawn.astype(out[name].dtype))
    for name, factor in factors.items():
        out[name] = (out[name] * factor).astype(out[name].dtype)
    return out
```

```python
import math
from contextlib import ExitStack

import numpy as np

import concourse.bass as bass
from concourse import mybir

D = 1024
SEQ, DEC = 1024, 32
T = SEQ + DEC
PAST = 512
CHUNK, WINDOW, HD, KVH = 64, 128, 64, 4
ROT, THETA = HD // 4, 500000.0
FF = 2816
EPS = 1e-6
P = 128
KC = D // P
NB = 3
BW = T // NB
CONV = 4
XPW = T + 2 * (CONV - 1)
SX0, SX1 = SEQ + CONV - 1, SEQ + 2 * (CONV - 1)
GROUPS = KVH
FFI = FF // P // 2
UW = 1024
KV_CACHED = CHUNK
KW = SEQ + KV_CACHED + DEC
AU = SEQ // CHUNK + 1
ASLOTS = AU + 3
SIDE_MM = 4 * 3 * KC * NB
START_MM, SLOT_MM = 28, 13
RING_A = 4

(V_G1, V_G2, V_W0, V_W1, V_W2, V_W3, V_CB, V_BR, V_BI, V_LAM, V_S0, V_S1, V_S2, V_H0, V_SP, V_NSP) = range(16)
NV_IN, NV = 14, 16
C_ID, C_ONE, C_BLK, C_PERM, C_VEC = 0, P, 2 * P, 3 * P, 4 * P
C_GAIN = C_VEC + KC * NV_IN
C_SINK = C_GAIN + 2
C_END = C_SINK + D // P
HT = 32


def unit_shape(u):
    if u == AU - 1:
        return DEC, KV_CACHED + DEC, SEQ
    return CHUNK, min(u + 1, 2) * CHUNK, u * CHUNK


class Count:

    def __init__(self):
        self.at, self.reg = 0, None

    def add(self, n=1):
        self.at += n

    def enter(self, reg, first, per):
        self.entry, self.first, self.per, self.reg = self.at, first, per, reg
        self.at -= per * first

    def leave(self, trips):
        assert self.at == self.entry - self.per * self.first + self.per, "the loop's body advances by `per`"
        self.at, self.reg = self.entry + self.per * trips, None

    def value(self, plus=0):
        return self.at + plus if self.reg is None else self.reg * self.per + (self.at + plus)


class Job:

    def __init__(self, bank, before, after, unit, done):
        self.bank, self.before, self.after, self.unit, self.done = bank, before, after, unit, done


class Plan:

    def __init__(self, job_done, unit_done):
        self.job_done, self.unit_done = job_done, unit_done
        self.uses = [Count() for _ in range(6)]
        self.jobs, self.units, self.bank, self.banks = Count(), Count(), 0, 6

    def ring(self, banks):
        self.bank, self.banks = 0, banks

    def take(self, last=False):
        b = self.bank
        self.bank = (b + 1) % self.banks
        u = self.uses[b]
        if last:
            done = (self.unit_done, self.units.value(1))
        else:
            done = (self.job_done, self.jobs.value(1))
        job = Job(b, u.value(), u.value(1), self.units.value(), done)
        u.add()
        (self.units if last else self.jobs).add()
        return job

    def loop(self, reg, first, jobs, units):
        for u in self.uses[:self.banks]:
            u.enter(reg, first, jobs // self.banks)
        self.jobs.enter(reg, first, jobs - units)
        self.units.enter(reg, first, units)

    def end(self, trips):
        for c in [*self.uses[:self.banks], self.jobs, self.units]:
            c.leave(trips)


def side_down(plan, k):
    return plan.take(last=k in (KC * NB - 5, KC * NB - 1))


def step_mm(i):
    return START_MM + SLOT_MM * i


L_FRONT = 6
N_UNITS = GROUPS * (L_FRONT + 2) + 2 + 2 + 2 + KC + (GROUPS - 1) * 6 + 4 + KC + FFI * 6
JOBS_L = 4 * NB + 4 * NB + KC * NB
JOBS_A = KC * NB + 2 * NB + 2 * NB
KVG_DMAS = 16 * 7
JOBS_F = 2 * (4 * NB + KC * NB)


def build(nc, small_in, x_in, cs_in, w_in, kc_in, vc_in, y_out, kp_out, vp_out, ks_out, vs_out, tail_out):
    f32, f32r = mybir.dt.float32, mybir.dt.float32r
    ALU, ACT, AX = mybir.AluOpType, mybir.ActivationFunctionType, mybir.AxisListType

    kt_dram = nc.dram_tensor("kt_scratch", [KVH * HD, KW], f32, kind="Internal").ap()
    v_dram = nc.dram_tensor("v_scratch", [T, KVH * HD], f32, kind="Internal").ap()
    mb_dram = nc.dram_tensor("mb_scratch", [KC, P, T], f32, kind="Internal").ap()
    ta_dram = nc.dram_tensor("ta_scratch", [KC, P, T], f32, kind="Internal").ap()

    def blk(n):
        return slice(n * BW, (n + 1) * BW)

    ctx = ExitStack()
    with ctx:
        def tensor(stack, name, shape, dt=f32):
            return stack.enter_context(nc.sbuf_tensor(name, shape, dt))

        def sem(name):
            return ctx.enter_context(nc.semaphore(name))

        small = tensor(ctx, "small", [P, C_END])
        vt = tensor(ctx, "vt", [P, KC, NV])
        nsink = tensor(ctx, "nsink", [P, D // P])
        wraw = tensor(ctx, "wraw", [P, 2, UW])
        wh = tensor(ctx, "wh", [P, 2, UW], f32r)
        wl = tensor(ctx, "wl", [P, 2, UW], f32r)
        acc = tensor(ctx, "acc", [P, KC, T])
        acth = tensor(ctx, "acth", [P, KC, T], f32r)
        actl = tensor(ctx, "actl", [P, KC, T], f32r)
        ident = small[:, C_ID:C_ID + P]
        ones = small[:, C_ONE:C_ONE + P]
        blkones = small[:, C_BLK:C_BLK + P]
        perm = small[:, C_PERM:C_PERM + P]
        vec_in = small[:, C_VEC:C_GAIN].rearrange("p (c k) -> p c k", k=NV_IN)
        sink = small[:, C_SINK:C_END]

        with ExitStack() as s:
            xsq = tensor(s, "xsq", [P, 2, 4, BW])
            xstd = tensor(s, "xstd", [P, 2, BW])
            x32 = tensor(s, "x32", [P, 4, BW])
            spt = tensor(s, "spt", [P, 6, KC])
        with ExitStack() as s:
            vg = tensor(s, "vg", [P, 2, NV])
            xp = tensor(s, "xp", [P, 2, XPW])
            xc = tensor(s, "xc", [P, 2, T])
            ti = tensor(s, "ti", [P, 2, T])
            aa = tensor(s, "aa", [P, 2, T])
            gel = tensor(s, "gel", [P, 2, T])
            xch = tensor(s, "xch", [P, 2, T], f32r)
            xcl = tensor(s, "xcl", [P, 2, T], f32r)
            ph = tensor(s, "ph", [P, 2, T], f32r)
            pl = tensor(s, "pl", [P, 2, T], f32r)
            tail = tensor(s, "tail", [P, KC, 8])
            vst = tensor(s, "vst", [P, 2, KVH * HD])
        with ExitStack() as s:
            oh = tensor(s, "oh", [P, 2, T], f32r)
            ol = tensor(s, "ol", [P, 2, T], f32r)
            cs = tensor(s, "cs", [P, 2, T])
            kg = tensor(s, "kg", [P, 2, KW])
            vgr = tensor(s, "vgr", [P, AU, HD])
            qt = tensor(s, "qt", [P, 2 * T])
            qsb = tensor(s, "qsb", [P, 2, BW])
            qsq = tensor(s, "qsq", [P, 2, BW])
            qstd = tensor(s, "qstd", [P, 2, BW])
            rt1 = tensor(s, "rt1", [P, BW])
            rt2 = tensor(s, "rt2", [P, BW])
            kst = tensor(s, "kst", [P, 2, BW])
            tg = tensor(s, "tg", [P, 3, BW])
            pr = tensor(s, "pr", [P, 3, 2, P])
            pt = tensor(s, "pt", [P, 2, 2 * P])
            o32 = tensor(s, "o32", [P, 2, 2, CHUNK])
            snk = tensor(s, "snk", [P, 2, 2])
            sm = tensor(s, "sm", [P, 3, 6, 2])
        with ExitStack() as s:
            tensor(s, "hold", [P, 4, T])
            mg = tensor(s, "mg", [P, 5, 2, T])
        n2h = tensor(ctx, "n2h", [P, KC, T], f32r)
        n2l = tensor(ctx, "n2l", [P, KC, T], f32r)
        ssum = tensor(ctx, "ssum", [P, T])
        with ExitStack() as s:
            xr = tensor(s, "xr", [P, NB, BW])
            x1sq = tensor(s, "x1sq", [P, 2, BW])
        with ExitStack() as s:
            sg = tensor(s, "sg", [P, NB, BW])
            tu = tensor(s, "tu", [P, 2, BW])
        hh = acth[:, 0:4, :].rearrange("p (s c) t -> p s c t", s=2)
        hl = actl[:, 0:4, :].rearrange("p (s c) t -> p s c t", s=2)

        bank = [ctx.enter_context(nc.psum_tensor(f"bank{i}", [P, 512], f32)) for i in range(8)]
        aux0, aux1 = bank[6], bank[7]
        sbank = bank[RING_A:RING_A + 2]

        small_in_s, x_in_s = sem("small_loaded"), [sem(f"x_loaded{n}") for n in range(NB)]
        raw_loaded = [sem(f"weights_loaded{i}") for i in range(2)]
        split_done, unit_done, job_done = sem("weights_split"), sem("unit_done"), sem("job_done")
        free = [sem(f"bank_free{i}") for i in range(6)]
        vec_done, sp_act = sem("vectors_done"), sem("softplus_exp")
        xsq_done, xss_done, xstd_done, xrec_done = sem("x_squared"), sem("x_sumsq"), sem("x_std"), sem("x_rstd")
        x32_done, xh_done, xl_done, zero_done = sem("x_normed"), sem("x_high"), sem("x_low"), sem("acc_zeroed")
        vg_done, pad_done, conv_done, tail_done = sem("lru_vectors"), sem("conv_pads"), sem("conv_taps"), sem("tails")
        xch_done, xcl_done, a_done, tau_done = sem("conv_high"), sem("conv_low"), sem("lru_a"), sem("lru_tau")
        ix_done, aa_done, msq_done, mult_done = sem("lru_gated_x"), sem("lru_a_squared"), sem("lru_mult_squared"), sem("lru_mult")
        one_done, b_done, h_done, prod_done = sem("lru_first_mult"), sem("lru_b"), sem("lru_h"), sem("lru_product")
        ph_done, pl_done = sem("product_high"), sem("product_low")
        v_stored, kv_stored, cs_loaded = [sem(f"v_stored{i}") for i in range(2)], sem("kv_stored"), sem("rope_loaded")
        ss_done, rot_done, std_done = sem("qk_sumsq"), sem("qk_rotated"), sem("qk_std")
        rot_used, t1_done, rsum_done, rrec_done, rh_done, rope_done = (
            sem("rope_sin"), sem("rope_cos"), sem("rope_sum"), sem("qk_rstd"), sem("rope_head0"), sem("rope_done"))
        k_stored = [sem(f"k_stored{i}") for i in range(2)]
        gb_done, mb_stored = sem("lru_gated"), [sem(f"mb_stored{i}") for i in range(2)]
        kvg_loaded, kz_done = sem("kv_group_loaded"), sem("key_zeros")
        snk_done = sem("sinks_done")
        s_done, t_done, o_done = sem("scores_done"), sem("probs_transposed"), sem("attended")
        mx_done, nm0_done, nm_done = sem("row_max"), sem("neg_max"), sem("sink_less_max")
        exp_done, den_done, rc_done, p_done = sem("exp_done"), sem("denominator"), sem("denominator_inverse"), sem("probs_done")
        pt_done, o32_done, oh_done, ol_done = sem("probs_t_copied"), sem("o_copied"), sem("o_high"), sem("o_low")
        ta_stored = [sem(f"ta_stored{i}") for i in range(NB)]
        mg_loaded = [sem(f"merge_loaded{i}") for i in range(5)]
        mg1_done, mg2_done, mh_done, ml_done = sem("merge_a"), sem("merged"), sem("merged_high"), sem("merged_low")
        xr_loaded = [sem(f"x_again{n}") for n in range(NB)]
        x1_done, n2h_done, x1sq_done, n2l_done, ssum_done = sem("x1_done"), sem("n2_high"), sem("x1_squared"), sem("n2_low"), sem("x1_sumsq")
        ssall_done, std2_done, rstd2_done = sem("x1_sumsq_all"), sem("x1_std"), sem("x1_rstd")
        gate_done, silu_done, up_done, h32_done, hh_done, hl_done = (
            sem("gate_scaled"), sem("silu_done"), sem("up_scaled"), sem("hidden"), sem("hidden_high"), sem("hidden_low"))
        y_done, stored = sem("y_done"), sem("outputs_stored")
        block = ctx.enter_context(nc.Block())

        def wait(eng, s, value):
            if isinstance(value, int):
                if value > 0:
                    eng.wait_ge(s, value)
            else:
                v = eng.to_reg(value) if eng is nc.gpsimd else eng.snap(value)
                eng.wait_ge(small_in_s, 16)
                eng.wait_ge(s, v)

        @block.gpsimd
        def _(pool):
            def split(i, u, first):
                wait(pool, raw_loaded[u], 16 * i + 16)
                if not first:
                    wait(pool, unit_done, 2 * i + u - 1)
                nc.gpsimd.tensor_scalar(wh[:, u, :], wraw[:, u, :], 1.0, 0.0, ALU.mult, ALU.add).then_inc(split_done, 1)
                wait(pool, split_done, 4 * i + 2 * u + 1)
                nc.gpsimd.tensor_tensor(wl[:, u, :], wraw[:, u, :], wh[:, u, :].bitcast(f32), ALU.subtract)\
                    .then_inc(split_done, 1)

            for u in range(2):
                split(0, u, True)
            with pool.Fori(1, N_UNITS // 2) as i:
                for u in range(2):
                    split(i, u, False)

        @block.tensor
        def _(pe):
            plan = Plan(job_done, unit_done)

            def mm(*args, **kw):
                return nc.tensor.matmul(*args, **kw)

            def weights(slot_check=0):
                wait(pe, split_done, 2 * plan.units.value(1 + slot_check))

            def products(out, lhs, rhs, cols, first, last):
                mm(out, lhs[0], rhs[0][cols], start=first, stop=False)
                mm(out, lhs[0], rhs[1][cols], start=False, stop=False)
                return mm(out, lhs[1], rhs[0][cols], start=False, stop=last)

            def dense(slot, rh, rl, before=None, each=None):
                weights()
                for n in range(NB):
                    job = plan.take(last=n == NB - 1)
                    if before:
                        before(n)
                    wait(pe, free[job.bank], job.before)
                    out = bank[job.bank][:, 0:BW]
                    for k in range(KC):
                        w = slice(k * P, (k + 1) * P)
                        i1 = mm(out, wh[:, slot, w], rh[:, k, blk(n)], start=k == 0, stop=False)
                        if each:
                            each()
                        i2 = mm(out, wh[:, slot, w], rl[:, k, blk(n)], start=False, stop=False)
                        if each:
                            each()
                        i3 = mm(out, wl[:, slot, w], rh[:, k, blk(n)], start=False, stop=k == KC - 1)
                        if k == KC - 1:
                            i3.then_inc(job.done[0], 1)
                        if each:
                            each()

            def down(rh, rl, after_first=None):
                for half in range(2):
                    weights()
                    for ml in range(4):
                        for n in range(NB):
                            job = plan.take(last=ml == 3 and n == NB - 1)
                            wait(pe, free[job.bank], job.before)
                            out = bank[job.bank][:, 0:BW]
                            for k in range(2):
                                w = slice(k * 512 + ml * P, k * 512 + (ml + 1) * P)
                                mm(out, wh[:, half, w], rh[:, k, blk(n)], start=k == 0, stop=False)
                                mm(out, wh[:, half, w], rl[:, k, blk(n)], start=False, stop=False)
                                i3 = mm(out, wl[:, half, w], rh[:, k, blk(n)], start=False, stop=k == 1)
                            i3.then_inc(job.done[0], 1)
                        if half == 0 and ml == 0 and after_first:
                            after_first()

            pe.wait_ge(small_in_s, 16)
            for n in range(NB):
                if n == 2:
                    pe.wait_ge(xstd_done, 1)
                for half in range(2):
                    pe.wait_ge(xsq_done, 2 * n + half + 1)
                    for c in range(4):
                        i = mm((aux0, aux1)[n % 2][:, 0:BW], ones, xsq[:, half, c, :],
                               start=half == 0 and c == 0, stop=half == 1 and c == 3)
                    i.then_inc(xss_done, 1)

            def lru_front(g, first):
                for i in range(4):
                    dense(i % 2, acth, actl,
                          (lambda n: pe.wait_ge(xl_done, KC * (n + 1))) if first and i == 0 else None)
                for i in range(2):
                    weights()
                    wait(pe, xcl_done, 2 * g + i + 1)
                    for gate in range(2):
                        for n in range(NB):
                            job = plan.take(last=gate == 1 and n == NB - 1)
                            wait(pe, free[job.bank], job.before)
                            out, w = bank[job.bank][:, 0:BW], slice(gate * P, (gate + 1) * P)
                            mm(out, wh[:, i, w], xch[:, i, blk(n)], start=True, stop=False)
                            mm(out, wh[:, i, w], xcl[:, i, blk(n)], start=False, stop=False)
                            mm(out, wl[:, i, w], xch[:, i, blk(n)], start=False, stop=True).then_inc(job.done[0], 1)

            def lru_down(g):
                wait(pe, pl_done, 2 * g + 2)
                down(ph, pl)

            lru_front(0, True)
            with pe.Fori(1, GROUPS) as g:
                plan.loop(g, 1, JOBS_L, L_FRONT + 2)
                lru_front(g, False)
                lru_down(g - 1)
            plan.end(GROUPS - 1)

            weights(1)
            for t in range(9):
                if t == 8:
                    plan.units.add()
                job = plan.take(last=t == 8)
                wait(pe, free[job.bank], job.before)
                out, c0 = bank[job.bank][:, 0:KVH * HD], min(t * P, T - P)
                for k in range(KC):
                    w, x = slice(k % 4 * 256, k % 4 * 256 + 256), slice(c0, c0 + P)
                    mm(out, acth[:, k, x], wh[:, k // 4, w], start=k == 0, stop=False)
                    mm(out, acth[:, k, x], wl[:, k // 4, w], start=False, stop=False)
                    i = mm(out, actl[:, k, x], wh[:, k // 4, w], start=False, stop=k == KC - 1)
                    if t == 8 and k == 3:
                        i.then_inc(unit_done, 1)
                i.then_inc(job.done[0], 1)
            lru_down(GROUPS - 1)

            def qk_aux(base, k, b, after):
                wait(pe, free[b], after)
                wait(pe, std_done, base + k)
                mm(aux0[:, 0:BW], blkones, qsq[:, k % 2, :], start=True, stop=True).then_inc(ss_done, 1)
                wait(pe, rot_used, base + k)
                mm(aux1[:, 0:BW], perm, qsb[:, k % 2, :], start=True, stop=True).then_inc(rot_done, 1)

            def qk(base, late=None):
                for i in range(2):
                    weights()
                    for n in range(NB):
                        job = plan.take(last=n == NB - 1)
                        wait(pe, free[job.bank], job.before)
                        out = bank[job.bank][:, 0:BW]
                        for k in range(KC):
                            w = slice(k * P, (k + 1) * P)
                            mm(out, wh[:, i, w], acth[:, k, blk(n)], start=k == 0, stop=False)
                            mm(out, wh[:, i, w], actl[:, k, blk(n)], start=False, stop=False)
                            i3 = mm(out, wl[:, i, w], acth[:, k, blk(n)], start=False, stop=k == KC - 1)
                        i3.then_inc(job.done[0], 1)
                        if late:
                            qk_aux(*late)
                        late = (base, NB * i + n, job.bank, job.after)
                return late

            late = qk(0)
            late = qk(6, late)

            for m in range(KC - 2):
                dense(m % 2, acth, actl)
                if m == 0:
                    qk_aux(*late)

            def attention_step(g, i):
                n0 = g * AU
                if i < AU and i >= 2:
                    wait(pe, exp_done, n0 + i - 1)
                if 0 <= i - 3 < AU:
                    wait(pe, pt_done, n0 + i - 2)
                    if i >= 4:
                        wait(pe, o32_done, n0 + i - 3)
                if 0 <= i - 2 < AU:
                    wait(pe, p_done, n0 + i - 1)
                if i < AU:
                    q, k, q0 = unit_shape(i)
                    k0 = q0 + q - k if i < AU - 1 else SEQ
                    mm(sbank[i % 2][0:2 * q, 0:2 * P].rearrange("p (h k) -> p h k", h=2)[:, :, 0:k],
                       qt[:, 2 * q0:2 * (q0 + q)], kg[:, :, k0:k0 + k], start=True, stop=True).then_inc(s_done, 1)
                if 0 <= i - 3 < AU:
                    q, k, _ = unit_shape(i - 3)
                    for h in range(2):
                        x = mm(aux0[h * HD:(h + 1) * HD, 0:2 * q], vgr[0:k, i - 3, :],
                               pt[0:k, (i - 3) % 2, h * 2 * q:(h + 1) * 2 * q], start=True, stop=True)
                    x.then_inc(o_done, 1)
                if 0 <= i - 2 < AU:
                    q, k, _ = unit_shape(i - 2)
                    for h in range(2):
                        x = nc.tensor.transpose(aux1[0:k, h * 2 * q:(h + 1) * 2 * q], pr[0:2 * q, (i - 2) % 3, h, 0:k],
                                                ident[0:2 * q, 0:2 * q])
                    x.then_inc(t_done, 1)

            def down_blocks(rh, rl, each):
                weights(1)
                for n in range(NB):
                    for m in range(KC):
                        job = side_down(plan, n * KC + m)
                        wait(pe, free[job.bank], job.before)
                        out = bank[job.bank][:, 0:BW]
                        for k in range(2):
                            w = slice(k * 512 + m % 4 * P, k * 512 + (m % 4 + 1) * P)
                            mm(out, wh[:, m // 4, w], rh[:, k, blk(n)], start=k == 0, stop=False)
                            each()
                            mm(out, wh[:, m // 4, w], rl[:, k, blk(n)], start=False, stop=False)
                            each()
                            i3 = mm(out, wl[:, m // 4, w], rh[:, k, blk(n)], start=False, stop=k == 1)
                            if k == 1:
                                i3.then_inc(job.done[0], 1)
                            each()

            def group(g, first, last):
                done = [0, 0]
                b = (plan.bank - 1) % RING_A
                late = (6 * g + 6, 5, b, plan.uses[b].value())

                def each():
                    done[0] += 1
                    if done[0] == START_MM // 2 and not first:
                        qk_aux(*late)
                    if done[1] < ASLOTS and done[0] == step_mm(done[1]):
                        if done[1] == 0:
                            wait(pe, rope_done, 6 * g + 12)
                            wait(pe, kvg_loaded, KVG_DMAS * (g + 1))
                            wait(pe, kz_done, 2)
                        attention_step(g, done[1])
                        done[1] += 1

                if first:
                    for i in range(2):
                        dense(i, acth, actl, None, each)
                else:
                    wait(pe, ol_done, AU * g)
                    down_blocks(oh, ol, each)
                for i in range(2):
                    dense(i, acth, actl, None, each)
                assert done[1] == ASLOTS and done[0] == SIDE_MM
                if last:
                    plan.ring(6)
                    wait(pe, ol_done, AU * (g + 1))
                    down(oh, ol)
                else:
                    wait(pe, pt_done, AU * (g + 1))
                    wait(pe, o32_done, AU * (g + 1))
                    qk(6 * g + 12)

            for b in (RING_A, RING_A + 1):
                pe.wait_ge(free[b], plan.uses[b].value())
            plan.ring(RING_A)
            group(0, True, False)
            with pe.Fori(1, GROUPS - 1) as g:
                plan.loop(g, 1, JOBS_A, 6)
                group(g, False, False)
            plan.end(GROUPS - 2)
            group(GROUPS - 1, False, True)

            pe.wait_ge(ml_done, KC)
            with pe.Fori(0, KC // 2) as i:
                plan.loop(i, 0, 2 * NB, 2)
                for slot in range(2):
                    dense(slot, acth, actl)
            plan.end(KC // 2)

            def sumsq2():
                for n in range(NB):
                    if n == 2:
                        pe.wait_ge(std2_done, 1)
                    mm((aux0, aux1)[n % 2][:, 0:BW], ones, ssum[:, blk(n)], start=True, stop=True).then_inc(ssall_done, 1)

            def ffn_front(first):
                for i in range(4):
                    dense(i % 2, n2h, n2l)
                    if first and i == 0:
                        pe.wait_ge(ssum_done, KC * NB)
                        sumsq2()

            def ffn_down(i, slot):
                wait(pe, hl_done, 6 * i + 6)
                down(hh[:, slot], hl[:, slot])

            pe.wait_ge(n2l_done, KC * NB)
            ffn_front(True)
            with pe.Fori(0, FFI // 2) as j:
                plan.loop(j, 0, JOBS_F, 12)
                for s in range(2):
                    ffn_front(False)
                    ffn_down(2 * j + s, s)
            plan.end(FFI // 2)
            ffn_down(FFI - 1, 0)
            assert plan.units.value() == N_UNITS

        @block.scalar
        def _(act):
            plan = Plan(job_done, unit_done)
            f = nc.scalar.activation

            act.dma_start(kt_dram[:, SEQ:SEQ + KV_CACHED], kc_in[:, WINDOW - KV_CACHED:WINDOW]).then_inc(kv_stored, 16)
            act.dma_start(ks_out[:, 0:WINDOW - DEC], kc_in[:, DEC:WINDOW]).then_inc(kv_stored, 16)
            act.dma_start(vs_out[0:WINDOW - DEC, :], vc_in[DEC:WINDOW, :]).then_inc(kv_stored, 16)

            act.wait_ge(small_in_s, 16)
            f(spt[:, 0, :], vec_in[:, :, V_LAM], ACT.Abs).then_inc(sp_act, 1)
            act.wait_ge(sp_act, 1)
            f(spt[:, 1, :], spt[:, 0, :], ACT.Exp, scale=-1.0).then_inc(sp_act, 1)
            for n in range(NB):
                act.wait_ge(x_in_s[n], 16)
                for half in range(2):
                    wait(act, xss_done, 2 * (n - 1) + half + 1)
                    f(xsq[:, half, :, :], acc[:, 4 * half:4 * half + 4, blk(n)], ACT.Square).then_inc(xsq_done, 1)
                act.wait_ge(xss_done, 2 * n + 2)
                wait(act, x32_done, KC * (n - 1))
                f(xstd[:, n % 2, :], (aux0, aux1)[n % 2][:, 0:BW], ACT.Sqrt, scale=1.0 / D, bias=EPS)\
                    .then_inc(xstd_done, 1)
                for c in range(KC):
                    act.wait_ge(x32_done, n * KC + c + 1)
                    f(acth[:, c, blk(n)], x32[:, c % 4, :], ACT.Copy).then_inc(xh_done, 1)

            def lru_front(g, first):
                for i in range(2):
                    if not first:
                        wait(act, msq_done, 2 * g + i - 1)
                    elif i == 0:
                        act.wait_ge(xl_done, KC * NB)
                    for n in range(NB):
                        job = plan.take(last=n == NB - 1)
                        wait(act, *job.done)
                        ps, c0 = bank[job.bank], CONV - 1 + n * BW
                        if n < NB - 1:
                            f(xp[:, i, c0:c0 + BW], ps[:, 0:BW], ACT.Copy).then_inc(free[job.bank], 1)
                        else:
                            f(xp[:, i, c0:SX0], ps[:, 0:BW - DEC], ACT.Copy)
                            f(xp[:, i, SX1:XPW], ps[:, BW - DEC:BW], ACT.Copy).then_inc(free[job.bank], 1)
                for i in range(2):
                    if not first:
                        wait(act, pl_done, 2 * g + i - 1)
                    for n in range(NB):
                        job = plan.take(last=n == NB - 1)
                        wait(act, *job.done)
                        f(gel[:, i, blk(n)], bank[job.bank][:, 0:BW], ACT.Gelu_apprx_tanh).then_inc(free[job.bank], 1)
                    wait(act, conv_done, 16 * g + 8 * i + 8)
                    f(xch[:, i, :], xc[:, i, :], ACT.Copy).then_inc(xch_done, 1)
                wait(act, vg_done, g + 1)
                for i in range(2):
                    wait(act, xcl_done, 2 * g + i + 1)
                    for gate in range(2):
                        for n in range(NB):
                            job = plan.take(last=gate == 1 and n == NB - 1)
                            wait(act, *job.done)
                            dst = (xp, ti)[gate][:, i, blk(n)]
                            f(dst, bank[job.bank][:, 0:BW], ACT.Tanh, scale=0.5,
                              bias=vg[:, i, V_BR + gate:V_BR + gate + 1]).then_inc(free[job.bank], 1)
                    wait(act, free[job.bank], job.after)
                    f(aa[:, i, :], xp[:, i, 0:T], ACT.Exp, scale=vg[:, i, V_NSP:V_NSP + 1],
                      bias=vg[:, i, V_NSP:V_NSP + 1]).then_inc(a_done, 1)
                    wait(act, a_done, 2 * g + i + 1)
                    f(xp[:, i, 0:T], xp[:, i, 0:T], ACT.Tanh, scale=vg[:, i, V_SP:V_SP + 1],
                      bias=vg[:, i, V_SP:V_SP + 1]).then_inc(tau_done, 1)
                for i in range(2):
                    wait(act, msq_done, 2 * g + i + 1)
                    f(xc[:, i, :], xc[:, i, :], ACT.Sqrt).then_inc(mult_done, 1)

            def lru_products(g):
                for i in range(2):
                    wait(act, prod_done, 2 * g + i + 1)
                    if i == 0:
                        wait(act, unit_done, plan.units.value())
                    f(ph[:, i, :], gel[:, i, :], ACT.Copy).then_inc(ph_done, 1)

            def skip_down():
                for k in range(2 * 4 * NB):
                    plan.take(last=k % (4 * NB) == 4 * NB - 1)

            lru_front(0, True)
            lru_products(0)
            with act.Fori(1, GROUPS) as g:
                plan.loop(g, 1, JOBS_L, L_FRONT + 2)
                lru_front(g, False)
                skip_down()
                lru_products(g)
            plan.end(GROUPS - 1)

            def store_v(t):
                act.wait_ge(free[vjobs[t].bank], vjobs[t].after)
                if t < 8:
                    act.dma_start(v_dram[t * P:(t + 1) * P, :], vst[:, t % 2, :]).then_inc(v_stored[t % 2], 16)
                else:
                    act.dma_start(v_dram[SEQ:T, :], vst[P - DEC:P, t % 2, :]).then_inc(v_stored[0], 16)
                    act.dma_start(vs_out[WINDOW - DEC:WINDOW, :], vst[P - DEC:P, 0, :]).then_inc(stored, 16)
                if t == 7:
                    act.dma_start(vp_out[:, :], vst[:, 1, :]).then_inc(stored, 16)

            vjobs = []
            for t in range(9):
                if t == 8:
                    plan.units.add()
                job = plan.take(last=t == 8)
                vjobs.append(job)
                act.wait_ge(*job.done)
                if t >= 2:
                    act.wait_ge(v_stored[t % 2], 16 * (t // 2))
                f(vst[:, t % 2, :], bank[job.bank][:, 0:KVH * HD], ACT.Copy).then_inc(free[job.bank], 1)
                if t >= 1:
                    store_v(t - 1)
            store_v(8)
            skip_down()
            act.wait_ge(tail_done, 6 * GROUPS)
            act.dma_start(tail_out, tail[:, :, :]).then_inc(stored, 16)
            act.wait_ge(unit_done, plan.units.value())
            act.wait_ge(v_stored[0], 16 * 5)
            act.wait_ge(v_stored[1], 16 * 4)
            act.wait_ge(stored, 16 * 3)
            act.dma_start(cs[:, :, :], cs_in).then_inc(cs_loaded, 16)

            def qk_copy(base, k, gain):
                job = plan.take(last=k % NB == NB - 1)
                wait(act, *job.done)
                wait(act, rot_done, base + k - 1)
                wait(act, t1_done, base + k - 1)
                f(qsq[:, k % 2, :], bank[job.bank][:, 0:BW], ACT.Square)
                f(qsb[:, k % 2, :], bank[job.bank][:, 0:BW], ACT.Identity, scale=gain).then_inc(free[job.bank], 1)

            def qk_root(base, k):
                wait(act, ss_done, base + k + 1)
                wait(act, rope_done, base + k - 1)
                f(qstd[:, k % 2, :], aux0[:, 0:BW], ACT.Sqrt, scale=1.0 / HD, bias=EPS).then_inc(std_done, 1)

            def store_k(k):
                act.wait_ge(rope_done, k + 1)
                n, slot, rows = k % NB, k % 2, slice(k // NB * P, (k // NB + 1) * P)
                if n < NB - 1:
                    act.dma_start(kt_dram[rows, blk(n)], kst[:, slot, :]).then_inc(k_stored[slot], 16)
                else:
                    a = SEQ - n * BW
                    act.dma_start(kt_dram[rows, n * BW:SEQ], kst[:, slot, 0:a]).then_inc(k_stored[slot], 16)
                    act.dma_start(kt_dram[rows, SEQ + KV_CACHED:KW], kst[:, slot, a:BW]).then_inc(k_stored[slot], 16)
                    act.dma_start(kp_out[rows, :], kst[:, slot, a - WINDOW:a]).then_inc(k_stored[slot], 16)
                    act.dma_start(ks_out[rows, WINDOW - DEC:WINDOW], kst[:, slot, a:BW]).then_inc(k_stored[slot], 16)

            qgain, kgain = small[:, C_GAIN:C_GAIN + 1], small[:, C_GAIN + 1:C_GAIN + 2]
            for k in range(6):
                qk_copy(0, k, kgain)
                if k >= 1:
                    qk_root(0, k - 1)
                if k >= 2:
                    store_k(k - 2)
            for k in range(6):
                qk_copy(6, k, qgain)
                if k == 0:
                    qk_root(0, 5)
                else:
                    qk_root(6, k - 1)
                if k < 2:
                    store_k(4 + k)

            def load_group(g):
                cols = bass.ds(g * HD, HD)
                lower = v_dram[0:SEQ - CHUNK, cols].rearrange("(u p) d -> p u d", p=CHUNK)
                upper = v_dram[CHUNK:SEQ, cols].rearrange("(u p) d -> p u d", p=CHUNK)
                for dst, src in ((kg[0:HD, 0, :], kt_dram[cols, :]),
                                 (kg[HD:P, 1, :], kt_dram[cols, :]),
                                 (vgr[0:CHUNK, 1:AU - 1, :], lower),
                                 (vgr[CHUNK:P, 1:AU - 1, :], upper),
                                 (vgr[0:CHUNK, 0, :], v_dram[0:CHUNK, cols]),
                                 (vgr[0:KV_CACHED, AU - 1, :], vc_in[WINDOW - KV_CACHED:WINDOW, cols]),
                                 (vgr[KV_CACHED:KV_CACHED + DEC, AU - 1, :], v_dram[SEQ:T, cols])):
                    act.dma_start(dst, src).then_inc(kvg_loaded, 16)

            def store_mb(m):
                act.wait_ge(gb_done, NB * (m + 1))
                act.dma_start(mb_dram[m], acc[:, m, :]).then_inc(mb_stored[m // 4], 16)

            def gate_b(m, n):
                job = plan.take(last=n == NB - 1)
                act.wait_ge(*job.done)
                wait(act, gb_done, NB * (m - 1) + n + 1)
                f(tg[:, n, :], bank[job.bank][:, 0:BW], ACT.Tanh, scale=0.5).then_inc(free[job.bank], 1)
                if m == 0 and n == 0:
                    qk_root(6, 5)
                if m >= 1 and n == 1:
                    store_mb(m - 1)

            for m in range(KC - 2):
                for n in range(NB):
                    gate_b(m, n)
                if m == 0:
                    act.wait_ge(k_stored[0], 16 * 6)
                    act.wait_ge(k_stored[1], 16 * 6)
                    act.wait_ge(kv_stored, 16 * 3)
                    load_group(0)

            def attention_step(g, i, read):
                n0 = g * AU
                if 0 <= i - 2 < AU:
                    q, k, _ = unit_shape(i - 2)
                    wait(act, t_done, n0 + i - 1)
                    if i >= 3:
                        wait(act, o_done, n0 + i - 3)
                    f(pt[0:k, i % 2, 0:4 * q], aux1[0:k, 0:4 * q], ACT.Copy).then_inc(pt_done, 1)
                if 0 <= i - 4 < AU:
                    q, _, q0 = unit_shape(i - 4)
                    if i - 4 in read:
                        wait(act, *read[i - 4])
                    wait(act, o32_done, n0 + i - 3)
                    f(oh[:, :, q0:q0 + q], o32[:, i % 2, :, 0:q], ACT.Copy).then_inc(oh_done, 1)
                if i < AU:
                    q, k, _ = unit_shape(i)
                    r = i % 3
                    wait(act, nm_done, n0 + i + 1)
                    if i >= 3:
                        wait(act, t_done, n0 + i - 2)
                    for h in range(2):
                        f(pr[0:2 * q, r, h, 0:k], sbank[i % 2][0:2 * q, h * P:h * P + k], ACT.Exp, scale=HD ** -0.5,
                          bias=sm[0:2 * q, r, 1, h:h + 1], accum_out=sm[0:2 * q, r, 3, h:h + 1])
                    f(sm[0:2 * q, r, 4, :], sm[0:2 * q, r, 2, :], ACT.Exp).then_inc(exp_done, 1)

            def group(g, first, last):
                jobs, read = [], {}
                if not first:
                    qk_root(6 * g + 6, 5)
                    down = [side_down(plan, k) for k in range(KC * NB)]
                    for n in range(NB):
                        read[max(-(-n * BW // CHUNK) - (n > 0), 0)] = down[(n + 1) * KC - 1].done

                def store_ta(j):
                    wait(act, free[jobs[j].bank], jobs[j].after)
                    act.dma_start(ta_dram[2 * g + j // NB, :, blk(j % NB)], tg[:, j % NB, :])\
                        .then_inc(ta_stored[j % NB], 16)

                def gate_a(j):
                    job = plan.take(last=j % NB == NB - 1)
                    jobs.append(job)
                    wait(act, *job.done)
                    if j >= NB:
                        wait(act, ta_stored[j % NB], 32 * g + 16)
                    elif first:
                        wait(act, gb_done, NB * (KC - 1) + j + 1)
                    f(tg[:, j % NB, :], bank[job.bank][:, 0:BW], ACT.Tanh, scale=0.5).then_inc(free[job.bank], 1)
                    if j == 0 and first:
                        store_mb(KC - 1)
                    if j >= 1:
                        store_ta(j - 1)

                side = [lambda j=j: gate_b(KC - 2 + j // NB, j % NB) for j in range(2 * NB)] if first else []
                side += [lambda j=j: gate_a(j) for j in range(2 * NB)]
                for i in range(ASLOTS + 2):
                    while side and (i >= ASLOTS or SIDE_MM - (len(side) - 1) * 3 * KC <= step_mm(i)):
                        side.pop(0)()
                    attention_step(g, i, read)
                store_ta(2 * NB - 1)
                if not last:
                    load_group(g + 1)
                    for k in range(6):
                        qk_copy(6 * g + 12, k, qgain)
                        if k >= 1:
                            qk_root(6 * g + 12, k - 1)
                    for n in range(NB):
                        wait(act, ta_stored[n], 32 * g + 32)

            plan.ring(RING_A)
            group(0, True, False)
            with act.Fori(1, GROUPS - 1) as g:
                plan.loop(g, 1, JOBS_A, 6)
                group(g, False, False)
            plan.end(GROUPS - 2)
            group(GROUPS - 1, False, True)
            plan.ring(6)
            skip_down()

            def load_merge(m):
                act.dma_start(mg[:, m % 5, 0, :], ta_dram[m]).then_inc(mg_loaded[m % 5], 16)
                act.dma_start(mg[:, m % 5, 1, :], mb_dram[m]).then_inc(mg_loaded[m % 5], 16)

            for n in range(NB):
                act.wait_ge(ta_stored[n], 16 * KC)
            for i in range(2):
                act.wait_ge(mb_stored[i], 16 * KC // 2)
            act.wait_ge(ol_done, AU * GROUPS)
            for m in range(5):
                load_merge(m)
            for n in range(NB):
                act.dma_start(xr[:, n, :], x_in[:, 0, blk(n)]).then_inc(xr_loaded[n], 16)
            for m in range(KC):
                act.wait_ge(mg2_done, m + 1)
                f(acth[:, m, :], mg[:, m % 5, 0, :], ACT.Copy).then_inc(mh_done, 1)
                if 1 <= m <= KC - 5:
                    act.wait_ge(ml_done, m)
                    load_merge(m + 4)

            def x1_parts(m, s, more):
                for n in range(NB):
                    job = plan.take(last=n == NB - 1)
                    wait(act, free[job.bank], job.after)
                    if more:
                        act.dma_start(xr[:, n, :], x_in[:, m + 1, blk(n)]).then_inc(xr_loaded[n], 16)
                    f(n2h[:, m, blk(n)], acc[:, m, blk(n)], ACT.Identity, scale=vt[:, m, V_G2:V_G2 + 1])\
                        .then_inc(n2h_done, 1)
                    f(x1sq[:, (s + n) % 2, :], acc[:, m, blk(n)], ACT.Square).then_inc(x1sq_done, 1)

            with act.Fori(0, KC // 2 - 1) as i:
                plan.loop(i, 0, 2 * NB, 2)
                for s in range(2):
                    x1_parts(2 * i + s, s, True)
            plan.end(KC // 2 - 1)
            for s in range(2):
                x1_parts(KC - 2 + s, s, s == 0)
            for n in range(NB):
                act.wait_ge(ssall_done, n + 1)
                f(ssum[:, blk(n)], (aux0, aux1)[n % 2][:, 0:BW], ACT.Sqrt, scale=1.0 / D, bias=EPS).then_inc(std2_done, 1)

            def ffn_front(i, slot):
                for c in range(2):
                    for n in range(NB):
                        job = plan.take(last=n == NB - 1)
                        wait(act, free[job.bank], job.after)
                        f(sg[:, n, :], sg[:, n, :], ACT.Silu).then_inc(silu_done, 1)
                    for n in range(NB):
                        plan.take(last=n == NB - 1)
                        wait(act, h32_done, 6 * i + NB * c + n + 1)
                        f(hh[:, slot, c, blk(n)], tu[:, (c + n) % 2, :], ACT.Copy).then_inc(hh_done, 1)

            ffn_front(0, 0)
            with act.Fori(0, FFI // 2) as j:
                plan.loop(j, 0, JOBS_F, 12)
                for s in range(2):
                    ffn_front(2 * j + 1 + s, 1 - s)
                    skip_down()
            plan.end(FFI // 2)

        final_jobs = []

        @block.vector
        def _(dve):
            plan = Plan(job_done, unit_done)
            V = nc.vector
            stt = V.scalar_tensor_tensor

            steps = [0]

            def vec(ins):
                ins.then_inc(vec_done, 1)
                steps[0] += 1
                dve.wait_ge(vec_done, steps[0])

            dve.wait_ge(small_in_s, 16)
            vec(V.tensor_copy(vt[:, :, 0:NV_IN], vec_in))
            vec(V.tensor_scalar(vt[:, :, V_BR:V_BI + 1], vec_in[:, :, V_BR:V_BI + 1], 0.5, None, ALU.mult))
            vec(V.tensor_scalar(nsink[:, :], sink, -1.0, None, ALU.mult))
            dve.wait_ge(sp_act, 2)
            e1, s1, s2, q1 = spt[:, 1, :], spt[:, 2, :], spt[:, 3, :], spt[:, 4, :]
            vec(V.tensor_scalar(s2, e1, 2.0, None, ALU.add))
            vec(V.reciprocal(q1, s2))
            vec(V.tensor_tensor(s1, e1, q1, ALU.mult))
            vec(V.tensor_tensor(s2, s1, s1, ALU.mult))
            vec(V.tensor_scalar(q1, s2, 1.0 / 15, None, ALU.mult))
            for n in (13, 11, 9, 7, 5, 3):
                vec(stt(q1, q1, 1.0 / n, s2, ALU.add, ALU.mult))
            vec(stt(q1, q1, 1.0, s1, ALU.add, ALU.mult))
            vec(V.tensor_scalar(s1, vec_in[:, :, V_LAM], -1.0, 0.0, ALU.mult, ALU.max))
            vec(stt(s1, q1, 2.0, s1, ALU.mult, ALU.add))
            vec(V.tensor_scalar(vt[:, :, V_SP], s1, 4.0, None, ALU.mult))
            vec(V.tensor_scalar(vt[:, :, V_NSP], s1, -4.0, None, ALU.mult))

            def x_low(i):
                dve.wait_ge(xh_done, i + 1)
                c, n = i % KC, i // KC
                V.tensor_tensor(actl[:, c, blk(n)], x32[:, c % 4, :], acth[:, c, blk(n)].bitcast(f32), ALU.subtract)\
                    .then_inc(xl_done, 1)

            for n in range(NB):
                dve.wait_ge(xstd_done, n + 1)
                V.reciprocal(xstd[:, n % 2, :], xstd[:, n % 2, :]).then_inc(xrec_done, 1)
                dve.wait_ge(xrec_done, n + 1)
                for c in range(KC):
                    i = n * KC + c
                    wait(dve, xl_done, i - 3)
                    stt(x32[:, c % 4, :], acc[:, c, blk(n)], vt[:, c, V_G1:V_G1 + 1], xstd[:, n % 2, :],
                        ALU.mult, ALU.mult).then_inc(x32_done, 1)
                    if i >= 1:
                        x_low(i - 1)
            x_low(KC * NB - 1)

            def skip(jobs, per_unit=NB):
                for n in range(jobs):
                    plan.take(last=n % per_unit == per_unit - 1)

            def add_down(half, ms=range(4)):
                for ml in ms:
                    for n in range(NB):
                        job = plan.take(last=ml == 3 and n == NB - 1)
                        wait(dve, *job.done)
                        a = acc[:, 4 * half + ml, blk(n)]
                        V.tensor_tensor(a, bank[job.bank][:, 0:BW], a, ALU.add).then_inc(free[job.bank], 1)
                return job

            def streams(i, j, src):
                return ((src[:, i, 0:SEQ], xp[:, i, j:j + SEQ]),
                        (src[:, i, SEQ:T], xp[:, i, SX0 + j:SX0 + j + DEC]))

            def lru_front(g, first):
                wait(dve, tau_done, 2 * g)
                V.tensor_copy(vg[:, :, :], vt[:, bass.ds(2 * g, 2), :]).then_inc(vg_done, 1)
                wait(dve, vg_done, g + 1)
                for i in range(2):
                    if not first:
                        wait(dve, msq_done, 2 * g + i - 1)
                    V.memset(xp[:, i, 0:CONV - 1], 0.0).then_inc(pad_done, 1)
                    V.tensor_copy(xp[:, i, SX0:SX1], vg[:, i, V_S0:V_S2 + 1]).then_inc(pad_done, 1)
                for i in range(2):
                    for n in range(NB):
                        job = plan.take(last=n == NB - 1)
                    jobs[i] = job
                for i in range(2):
                    wait(dve, free[jobs[i].bank], jobs[i].after)
                    wait(dve, pad_done, 4 * g + 2 * i + 2)
                    if not first:
                        wait(dve, pl_done, 2 * g + i - 1)
                    c0 = 16 * g + 8 * i
                    for j in range(CONV):
                        w = vg[:, i, V_W0 + j:V_W0 + j + 1]
                        for s, (dst, src) in enumerate(streams(i, j, xc)):
                            if j == 0:
                                V.tensor_scalar(dst, src, w, vg[:, i, V_CB:V_CB + 1], ALU.mult, ALU.add).then_inc(conv_done, 1)
                            else:
                                wait(dve, conv_done, c0 + 2 * j - 1 + s)
                                stt(dst, src, w, dst, ALU.mult, ALU.add).then_inc(conv_done, 1)
                    c = 2 * g + i
                    V.tensor_copy(tail[:, c, 0:3], xp[:, i, SEQ:SX0]).then_inc(tail_done, 1)
                    V.tensor_copy(tail[:, c, 3:6], xp[:, i, XPW - 3:XPW]).then_inc(tail_done, 1)
                    wait(dve, xch_done, c + 1)
                    V.tensor_tensor(xcl[:, i, :], xc[:, i, :], xch[:, i, :].bitcast(f32), ALU.subtract).then_inc(xcl_done, 1)
                skip(2 * NB)
                skip(4 * NB, 2 * NB)
                if first:
                    V.memset(acc[:, :, :], 0.0).then_inc(zero_done, 1)
                for i in range(2):
                    c = 2 * g + i
                    wait(dve, tau_done, c + 1)
                    stt(ti[:, i, :], ti[:, i, :], 1.0, xc[:, i, :], ALU.add, ALU.mult).then_inc(ix_done, 1)
                    wait(dve, ix_done, c + 1)
                    V.tensor_tensor(xc[:, i, :], aa[:, i, :], aa[:, i, :], ALU.mult).then_inc(aa_done, 1)
                    wait(dve, aa_done, c + 1)
                    stt(xc[:, i, :], xc[:, i, :], 1.0, xp[:, i, 0:T], ALU.add, ALU.mult).then_inc(msq_done, 1)

            def lru_scan(g, i):
                c = 2 * g + i
                wait(dve, mult_done, c + 1)
                V.memset(xc[:, i, 0:1], 1.0).then_inc(one_done, 1)
                wait(dve, one_done, c + 1)
                stt(ti[:, i, :], xc[:, i, :], 0.5, ti[:, i, :], ALU.mult, ALU.mult).then_inc(b_done, 1)
                wait(dve, b_done, c + 1)
                V.tensor_tensor_scan(xc[:, i, 0:SEQ], aa[:, i, 0:SEQ], ti[:, i, 0:SEQ], 0.0, ALU.mult, ALU.add)\
                    .then_inc(h_done, 1)
                V.tensor_tensor_scan(xc[:, i, SEQ:T], aa[:, i, SEQ:T], ti[:, i, SEQ:T], vg[:, i, V_H0:V_H0 + 1],
                                     ALU.mult, ALU.add).then_inc(h_done, 1)
                wait(dve, h_done, 2 * c + 2)
                V.tensor_copy(tail[:, c, 6:8], xc[:, i, SEQ - 1:T:DEC]).then_inc(tail_done, 1)
                V.tensor_tensor(gel[:, i, :], gel[:, i, :], xc[:, i, :], ALU.mult).then_inc(prod_done, 1)

            def lru_low(g):
                for i in range(2):
                    wait(dve, ph_done, 2 * g + i + 1)
                    V.tensor_tensor(pl[:, i, :], gel[:, i, :], ph[:, i, :].bitcast(f32), ALU.subtract).then_inc(pl_done, 1)

            jobs = [None, None]
            lru_front(0, True)
            lru_scan(0, 0)
            lru_scan(0, 1)
            lru_low(0)
            dve.wait_ge(zero_done, 1)
            with dve.Fori(1, GROUPS) as g:
                plan.loop(g, 1, JOBS_L, L_FRONT + 2)
                lru_front(g, False)
                add_down(0)
                lru_scan(g, 0)
                add_down(1)
                lru_scan(g, 1)
                lru_low(g)
            plan.end(GROUPS - 1)

            for t in range(9):
                if t == 8:
                    plan.units.add()
                plan.take(last=t == 8)
            add_down(0)
            add_down(1)

            def rope(base, k):
                x = blk(k % NB)
                wait(dve, rot_done, base + k + 1)
                wait(dve, rope_done, base + k)
                V.tensor_tensor(rt2[:, :], aux1[:, 0:BW], cs[:, 1, x], ALU.mult).then_inc(rot_used, 1)
                V.tensor_tensor(rt1[:, :], qsb[:, k % 2, :], cs[:, 0, x], ALU.mult).then_inc(t1_done, 1)
                wait(dve, rot_used, base + k + 1)
                wait(dve, t1_done, base + k + 1)
                V.tensor_tensor(rt1[:, :], rt1[:, :], rt2[:, :], ALU.add).then_inc(rsum_done, 1)
                wait(dve, std_done, base + k + 1)
                V.reciprocal(qstd[:, k % 2, :], qstd[:, k % 2, :]).then_inc(rrec_done, 1)
                wait(dve, rsum_done, base + k + 1)
                wait(dve, rrec_done, base + k + 1)

            def rope_k(k):
                rope(0, k)
                if k >= 2:
                    dve.wait_ge(k_stored[k % 2], 16 * {2: 1, 3: 1, 4: 5, 5: 2}[k])
                V.tensor_tensor(kst[:, k % 2, :], rt1[:, :], qstd[:, k % 2, :], ALU.mult).then_inc(rope_done, 1)

            def rope_q(base, k):
                rope(base, k)
                n = k % NB
                dst = qt[:, 2 * n * BW:2 * (n + 1) * BW].rearrange("p (b i t) -> p b i t", i=2, t=HT)
                V.tensor_tensor(dst[:, :, k // NB, :], rt1[:, :].rearrange("p (b t) -> p b t", t=HT),
                                qstd[:, k % 2, :].rearrange("p (b t) -> p b t", t=HT), ALU.mult).then_inc(rope_done, 1)

            dve.wait_ge(cs_loaded, 16)
            V.memset(kg[HD:P, 0, :], 0.0).then_inc(kz_done, 1)
            V.memset(kg[0:HD, 1, :], 0.0).then_inc(kz_done, 1)
            skip(4 * NB)
            for k in range(6):
                rope_k(k)
            for k in range(5):
                rope_q(6, k)

            def gated(m, n):
                job = plan.take(last=n == NB - 1)
                dve.wait_ge(free[job.bank], job.after)
                stt(acc[:, m, blk(n)], tg[:, n, :], 1.0, acc[:, m, blk(n)], ALU.add, ALU.mult).then_inc(gb_done, 1)

            for m in range(KC - 2):
                for n in range(NB):
                    gated(m, n)
                if m == 0:
                    rope_q(6, 5)

            def attention_step(g, i):
                n0 = g * AU
                if i < AU:
                    q, k, _ = unit_shape(i)
                    r = i % 3
                    rows = slice(0, 2 * q)
                    wait(dve, s_done, n0 + i + 1)
                    V.tensor_reduce(sm[rows, r, 0, :], sbank[i % 2][rows, 0:256].rearrange("p (h k) -> p h k", h=2)[:, :, 0:k],
                                    AX.X, ALU.max).then_inc(mx_done, 1)
                    wait(dve, mx_done, n0 + i + 1)
                    stt(sm[rows, r, 1, :], sm[rows, r, 0, :], -HD ** -0.5, snk[rows, 0, :], ALU.mult, ALU.min)\
                        .then_inc(nm0_done, 1)
                    wait(dve, nm0_done, n0 + i + 1)
                    V.tensor_tensor(sm[rows, r, 2, :], sm[rows, r, 1, :], snk[rows, 1, :], ALU.add).then_inc(nm_done, 1)
                if 0 <= i - 3 < AU:
                    q, _, _ = unit_shape(i - 3)
                    wait(dve, o_done, n0 + i - 2)
                    if i >= 5:
                        wait(dve, oh_done, n0 + i - 4)
                        wait(dve, ol_done, n0 + i - 4)
                    V.tensor_copy(o32[:, (i + 1) % 2, :, 0:q].rearrange("p i (b t) -> p b i t", t=HT),
                                  aux0[:, 0:2 * q].rearrange("p (b i t) -> p b i t", i=2, t=HT)).then_inc(o32_done, 1)
                if 0 <= i - 1 < AU:
                    q, k, _ = unit_shape(i - 1)
                    r, rows = (i - 1) % 3, slice(0, 2 * q)
                    wait(dve, exp_done, n0 + i)
                    V.tensor_tensor(sm[rows, r, 5, :], sm[rows, r, 3, :], sm[rows, r, 4, :], ALU.add).then_inc(den_done, 1)
                    wait(dve, den_done, n0 + i)
                    V.reciprocal(sm[rows, r, 5, :], sm[rows, r, 5, :]).then_inc(rc_done, 1)
                    wait(dve, rc_done, n0 + i)
                    V.tensor_tensor(pr[rows, r, :, 0:k], pr[rows, r, :, 0:k],
                                    sm[rows, r, 5, :].rearrange("p (h k) -> p h k", k=1).to_broadcast([2 * q, 2, k]),
                                    ALU.mult).then_inc(p_done, 1)
                if 0 <= i - 4 < AU:
                    q, _, q0 = unit_shape(i - 4)
                    wait(dve, oh_done, n0 + i - 3)
                    V.tensor_tensor(ol[:, :, q0:q0 + q], o32[:, i % 2, :, 0:q], oh[:, :, q0:q0 + q].bitcast(f32),
                                    ALU.subtract).then_inc(ol_done, 1)

            def group(g, first, last):
                if not first:
                    rope_q(6 * g + 6, 5)
                V.tensor_copy(snk[:, 0, :], nsink[:, bass.ds(2 * g, 2)]).then_inc(snk_done, 1)
                V.tensor_copy(snk[:, 1, :], sink[:, bass.ds(2 * g, 2)]).then_inc(snk_done, 1)
                wait(dve, snk_done, 2 * g + 2)
                if first:
                    side = [(3 * KC * (j + 1), lambda j=j: gated(KC - 2 + j // NB, j % NB)) for j in range(2 * NB)]
                else:
                    side = [(6 * (k + 1), lambda k=k: add_down_block(k)) for k in range(KC * NB)]
                for i in range(ASLOTS + 2):
                    while side and (i >= ASLOTS or side[0][0] <= step_mm(i)):
                        side.pop(0)[1]()
                    attention_step(g, i)
                skip(2 * NB)
                if first:
                    for half in range(2):
                        dve.wait_ge(mb_stored[half], 16 * 4)
                        V.memset(acc[:, 4 * half:4 * half + 4, :], 0.0).then_inc(zero_done, 1)
                    dve.wait_ge(zero_done, 3)
                if not last:
                    skip(2 * NB)
                    for k in range(5):
                        rope_q(6 * g + 12, k)

            def add_down_block(k):
                job = side_down(plan, k)
                wait(dve, *job.done)
                a = acc[:, k % KC, blk(k // KC)]
                V.tensor_tensor(a, bank[job.bank][:, 0:BW], a, ALU.add).then_inc(free[job.bank], 1)

            plan.ring(RING_A)
            group(0, True, False)
            with dve.Fori(1, GROUPS - 1) as g:
                plan.loop(g, 1, JOBS_A, 6)
                group(g, False, False)
            plan.end(GROUPS - 2)
            group(GROUPS - 1, False, True)
            plan.ring(6)

            def merge_low(m):
                dve.wait_ge(mh_done, m + 1)
                V.tensor_tensor(actl[:, m, :], mg[:, m % 5, 0, :], acth[:, m, :].bitcast(f32), ALU.subtract)\
                    .then_inc(ml_done, 1)

            for m in range(KC):
                job = add_down(m // 4, [m % 4])
                dve.wait_ge(free[job.bank], job.after)
                dve.wait_ge(mg_loaded[m % 5], 32 * (m // 5 + 1))
                stt(mg[:, m % 5, 0, :], mg[:, m % 5, 0, :], 1.0, acc[:, m, :], ALU.add, ALU.mult).then_inc(mg1_done, 1)
                if m >= 1:
                    merge_low(m - 1)
                dve.wait_ge(mg1_done, m + 1)
                V.tensor_tensor(mg[:, m % 5, 0, :], mg[:, m % 5, 0, :], mg[:, m % 5, 1, :], ALU.add).then_inc(mg2_done, 1)
            V.memset(ssum[:, :], 0.0).then_inc(zero_done, 1)
            merge_low(KC - 1)
            dve.wait_ge(zero_done, 4)

            def x1_low(m, n, s):
                wait(dve, n2h_done, NB * m + n + 1)
                stt(n2l[:, m, blk(n)], acc[:, m, blk(n)], vt[:, m, V_G2:V_G2 + 1], n2h[:, m, blk(n)].bitcast(f32),
                    ALU.mult, ALU.subtract).then_inc(n2l_done, 1)
                wait(dve, x1sq_done, NB * m + n + 1)
                V.tensor_tensor(ssum[:, blk(n)], ssum[:, blk(n)], x1sq[:, (s + n) % 2, :], ALU.add).then_inc(ssum_done, 1)

            with dve.Fori(0, KC // 2) as i:
                plan.loop(i, 0, 2 * NB, 2)
                for s in range(2):
                    m = 2 * i + s
                    for n in range(NB):
                        job = plan.take(last=n == NB - 1)
                        wait(dve, *job.done)
                        wait(dve, xr_loaded[n], 16 * m + 16)
                        stt(acc[:, m, blk(n)], bank[job.bank][:, 0:BW], 0.5, xr[:, n, :], ALU.mult, ALU.add)\
                            .then_inc(free[job.bank], 1)
                        if n >= 1:
                            x1_low(m, n - 1, s)
                    x1_low(m, NB - 1, s)
            plan.end(KC // 2)
            for n in range(NB):
                dve.wait_ge(std2_done, n + 1)
                V.reciprocal(ssum[:, blk(n)], ssum[:, blk(n)]).then_inc(rstd2_done, 1)

            def ffn_front(i, slot):
                for c in range(2):
                    b0 = 6 * i + NB * c
                    for n in range(NB):
                        job = plan.take(last=n == NB - 1)
                        wait(dve, *job.done)
                        wait(dve, h32_done, b0 + n - 2)
                        wait(dve, rstd2_done, n + 1)
                        V.tensor_tensor(sg[:, n, :], bank[job.bank][:, 0:BW], ssum[:, blk(n)], ALU.mult)\
                            .then_inc(free[job.bank], 1)

                    def low(n):
                        wait(dve, hh_done, b0 + n + 1)
                        V.tensor_tensor(hl[:, slot, c, blk(n)], tu[:, (c + n) % 2, :],
                                        hh[:, slot, c, blk(n)].bitcast(f32), ALU.subtract).then_inc(hl_done, 1)

                    for n in range(NB):
                        job = plan.take(last=n == NB - 1)
                        b = (c + n) % 2
                        wait(dve, *job.done)
                        wait(dve, hl_done, b0 + n - 1)
                        V.tensor_tensor(tu[:, b, :], bank[job.bank][:, 0:BW], ssum[:, blk(n)], ALU.mult)\
                            .then_inc(free[job.bank], 1)
                        wait(dve, free[job.bank], job.after)
                        wait(dve, silu_done, b0 + n + 1)
                        V.tensor_tensor(tu[:, b, :], tu[:, b, :], sg[:, n, :], ALU.mult).then_inc(h32_done, 1)
                        if n >= 1:
                            low(n - 1)
                    low(NB - 1)

            ffn_front(0, 0)
            with dve.Fori(0, FFI // 2) as j:
                plan.loop(j, 0, JOBS_F, 12)
                for s in range(2):
                    ffn_front(2 * j + 1 + s, 1 - s)
                    add_down(0)
                    add_down(1)
            plan.end(FFI // 2)
            for m in range(KC):
                start = plan.bank
                add_down(m // 4, [m % 4])
                last = (start + NB - 1) % 6
                final_jobs.append((last, plan.uses[last].value()))

        @block.sync
        def _(sp):
            sp.dma_start(small[:, :], small_in).then_inc(small_in_s, 16)
            sp.dma_start(acc[:, :, blk(0)], x_in[:, :, blk(0)]).then_inc(x_in_s[0], 16)
            for u in range(2):
                sp.dma_start(wraw[:, u, :], w_in[u]).then_inc(raw_loaded[u], 16)
            for n in range(1, NB):
                sp.dma_start(acc[:, :, blk(n)], x_in[:, :, blk(n)]).then_inc(x_in_s[n], 16)
            with sp.Fori(1, N_UNITS // 2) as i:
                for u in range(2):
                    wait(sp, split_done, 4 * i + 2 * u - 2)
                    sp.dma_start(wraw[:, u, :], w_in[2 * i + u]).then_inc(raw_loaded[u], 16)
            for m in range(KC):
                b, uses = final_jobs[m]
                sp.wait_ge(free[b], uses)
                sp.dma_start(y_out[m], acc[:, m, :]).then_inc(stored, 16)
            sp.wait_ge(stored, 16 * (KC + 3))
            for i in range(2):
                sp.wait_ge(k_stored[i], 16 * 6)
                sp.wait_ge(mb_stored[i], 16 * 4)
                sp.wait_ge(v_stored[i], 16 * (5 - i))
            for n in range(NB):
                sp.wait_ge(ta_stored[n], 16 * KC)
            sp.wait_ge(kv_stored, 16 * 3)




def weight_units(w):
    w_in, wao, wlo, wo = w["w_in"][0], w["w_attn_out"][0], w["w_lru_out"][0], w["w_o"][0]
    wgu, wd, wr, wi = w["w_gate_up"][0], w["w_down"][0], w["w_rg"][0], w["w_ig"][0]
    q0, k0, v0, x0, y0, a0 = 0, D, D + KVH * HD, D + 2 * KVH * HD, 2 * D + 2 * KVH * HD, 3 * D + 2 * KVH * HD
    b0 = a0 + D

    def cols(m, c0):
        return m[:, c0:c0 + P].reshape(KC, P, P).transpose(1, 0, 2).reshape(P, UW)

    def rows(m, pair):
        part = m[pair * 2 * P:(pair + 1) * 2 * P].reshape(2, P, 2, 512)
        return [part[:, :, h].transpose(1, 0, 2).reshape(P, UW) for h in range(2)]

    def gates(c):
        out = np.zeros((P, UW), w_in.dtype)
        for b in range(2):
            r = slice(b * HD, (b + 1) * HD)
            out[r, b * HD:(b + 1) * HD] = wr[2 * c + b]
            out[r, P + b * HD:P + (b + 1) * HD] = wi[2 * c + b]
        return out

    def front(g):
        return ([cols(w_in, x0 + (2 * g + i) * P) for i in range(2)] + [cols(w_in, y0 + (2 * g + i) * P) for i in range(2)]
                + [gates(2 * g + i) for i in range(2)])

    def queries(g):
        return [cols(w_in, q0 + (2 * g + i) * P) for i in range(2)]

    def hidden(i):
        return [cols(wgu, h * FF + (2 * i + c) * P) for c in range(2) for h in range(2)]

    units = front(0)
    for g in range(1, GROUPS):
        units += front(g) + rows(wlo, g - 1)
    units += [w_in[h * 512:(h + 1) * 512, v0:v0 + KVH * HD].reshape(4, P, KVH * HD).transpose(1, 0, 2).reshape(P, UW)
              for h in range(2)]
    units += rows(wlo, GROUPS - 1)
    units += [cols(w_in, k0 + i * P) for i in range(2)] + queries(0)
    units += [cols(w_in, b0 + m * P) for m in range(KC)]
    for g in range(GROUPS):
        if g:
            units += rows(wao, g - 1)
        units += [cols(w_in, a0 + (2 * g + i) * P) for i in range(2)]
        if g < GROUPS - 1:
            units += queries(g + 1)
    units += rows(wao, GROUPS - 1)
    units += [cols(wo, m * P) for m in range(KC)]
    units += hidden(0)
    for i in range(1, FFI):
        units += hidden(i) + rows(wd, i - 1)
    units += rows(wd, FFI - 1)
    return np.stack(units)


def by_feature(a):
    a = np.moveaxis(a, -1, 0)
    return np.moveaxis(a.reshape((KC, P) + a.shape[1:]), 0, 1)


def rope_tables():
    freqs = np.float32(THETA) ** (-np.arange(0, ROT, 2, dtype=np.float32) / np.float32(ROT))
    pos = np.concatenate([np.arange(SEQ), PAST + np.arange(DEC)]).astype(np.float32)
    ang = freqs[:, None] * pos[None, :]
    cos, sin = np.ones((HD, T), np.float32), np.zeros((HD, T), np.float32)
    cos[:ROT], sin[:ROT] = np.tile(np.cos(ang), (2, 1)), np.tile(np.sin(ang), (2, 1))
    return np.stack([np.tile(cos, (2, 1)), np.tile(sin, (2, 1))], 1)


def constants():
    blk, perm = np.zeros((P, P), np.float32), np.zeros((P, P), np.float32)
    for h in range(2):
        b = h * HD
        blk[b:b + HD, b:b + HD] = 1
        for d in range(ROT // 2):
            perm[b + ROT // 2 + d, b + d] = -1
            perm[b + d, b + ROT // 2 + d] = 1
    return [np.eye(P, dtype=np.float32), np.ones((P, P), np.float32), blk, perm]


def kernel(**inputs):
    import concourse.bacc as _bacc
    from concourse.bass_utils import run_bass_kernel_spmd as _run

    a = {k: np.asarray(v) for k, v in inputs.items()}
    x = np.concatenate([a["x_prompt"][0], a["x_sample"][0]], 0)
    vectors = np.stack([a["attn_norm"][0], a["ffn_norm"][0], *a["conv_w"][0], a["conv_b"][0], a["b_rg"][0], a["b_ig"][0],
                        a["lru_lambda"][0], *a["state_conv"][0, 0], a["state_lru"][0, 0]])
    sinks = np.tile(np.repeat(a["sinks"][0].reshape(GROUPS, 2, 2).transpose(1, 0, 2).reshape(2, 8), HT, 0), (2, 1))
    gains = np.stack([np.tile(a["q_norm"][0], 2), np.tile(a["k_norm"][0], 2)], 1)
    small = np.concatenate(constants() + [by_feature(vectors).reshape(P, KC * NV_IN), gains, sinks], 1)
    arrays = {
        "small": small,
        "x": np.ascontiguousarray(by_feature(x)),
        "rope": rope_tables(),
        "weights": weight_units(a),
        "cache_k": np.ascontiguousarray(a["cache_k"][0, 0].reshape(WINDOW, KVH * HD).T),
        "cache_v": np.ascontiguousarray(a["cache_v"][0, 0].reshape(WINDOW, KVH * HD)),
    }
    outs = {"y": (KC, P, T), "kp": (KVH * HD, WINDOW), "vp": (WINDOW, KVH * HD), "ks": (KVH * HD, WINDOW),
            "vs": (WINDOW, KVH * HD), "tail": (P, KC, 8)}

    nc = _bacc.Bacc("TRN2", target_bir_lowering=False, num_devices=1)
    args = [nc.dram_tensor(f"in_{k}", v.shape, mybir.dt.float32, kind="ExternalInput").ap() for k, v in arrays.items()]
    args += [nc.dram_tensor(f"out_{k}", s, mybir.dt.float32, kind="ExternalOutput").ap() for k, s in outs.items()]
    build(nc, *args)
    r = _run(nc, [{f"in_{k}": v for k, v in arrays.items()}], core_ids=[0]).results[0]

    y = np.ascontiguousarray(np.asarray(r["out_y"]).reshape(D, T).T)
    cache = (1, 1, WINDOW, KVH, HD)
    keys = [np.ascontiguousarray(np.asarray(r[k]).T).reshape(cache) for k in ("out_kp", "out_ks")]
    tail = np.asarray(r["out_tail"]).transpose(2, 1, 0).reshape(8, D)
    return (y[None, :SEQ], y[None, SEQ:],
            keys[0], np.asarray(r["out_vp"]).reshape(cache), tail[None, None, 0:3], tail[None, 6:7],
            keys[1], np.asarray(r["out_vs"]).reshape(cache), tail[None, None, 3:6], tail[None, 7:8])
```

```python
import math
from contextlib import ExitStack

import numpy as np

import concourse.bass as bass
from concourse import mybir

D = 1024
SEQ, DEC = 1024, 32
T = SEQ + DEC
PAST = 512
CHUNK, WINDOW, HD, KVH = 64, 128, 64, 4
ROT, THETA = HD // 4, 500000.0
FF = 2816
EPS = 1e-6
P = 128
KC = D // P
NB = 3
BW = T // NB
CONV = 4
XPW = T + 2 * (CONV - 1)
SX0, SX1 = SEQ + CONV - 1, SEQ + 2 * (CONV - 1)
GROUPS = KVH
FFI = FF // P // 2
UW = 1024
KV_CACHED = CHUNK
KW = SEQ + KV_CACHED + DEC
AU = SEQ // CHUNK + 1
ASLOTS = AU + 3
SIDE_MM = 4 * 3 * KC * NB
START_MM, SLOT_MM = 72, 11
RING_A = 4

(V_G1, V_G2, V_W0, V_W1, V_W2, V_W3, V_CB, V_BR, V_BI, V_LAM, V_S0, V_S1, V_S2, V_H0, V_SP, V_NSP) = range(16)
NV_IN, NV = 14, 16
C_ID, C_ONE, C_BLK, C_PERM, C_VEC = 0, P, 2 * P, 3 * P, 4 * P
C_GAIN = C_VEC + KC * NV_IN
C_SINK = C_GAIN + 2
C_END = C_SINK + D // P
HT = 32


def unit_shape(u):
    if u == AU - 1:
        return DEC, KV_CACHED + DEC, SEQ
    return CHUNK, min(u + 1, 2) * CHUNK, u * CHUNK


class Count:

    def __init__(self):
        self.at, self.reg = 0, None

    def add(self, n=1):
        self.at += n

    def enter(self, reg, first, per):
        self.entry, self.first, self.per, self.reg = self.at, first, per, reg
        self.at -= per * first

    def leave(self, trips):
        assert self.at == self.entry - self.per * self.first + self.per, "the loop's body advances by `per`"
        self.at, self.reg = self.entry + self.per * trips, None

    def value(self, plus=0):
        return self.at + plus if self.reg is None else self.reg * self.per + (self.at + plus)


class Job:

    def __init__(self, bank, before, after, unit, done):
        self.bank, self.before, self.after, self.unit, self.done = bank, before, after, unit, done


class Plan:

    def __init__(self, job_done, unit_done):
        self.job_done, self.unit_done = job_done, unit_done
        self.uses = [Count() for _ in range(6)]
        self.jobs, self.units, self.bank, self.banks = Count(), Count(), 0, 6

    def ring(self, banks):
        self.bank, self.banks = 0, banks

    def take(self, last=False):
        b = self.bank
        self.bank = (b + 1) % self.banks
        u = self.uses[b]
        if last:
            done = (self.unit_done, self.units.value(1))
        else:
            done = (self.job_done, self.jobs.value(1))
        job = Job(b, u.value(), u.value(1), self.units.value(), done)
        u.add()
        (self.units if last else self.jobs).add()
        return job

    def loop(self, reg, first, jobs, units):
        for u in self.uses[:self.banks]:
            u.enter(reg, first, jobs // self.banks)
        self.jobs.enter(reg, first, jobs - units)
        self.units.enter(reg, first, units)

    def end(self, trips):
        for c in [*self.uses[:self.banks], self.jobs, self.units]:
            c.leave(trips)


def side_down(plan, k):
    return plan.take(last=k in (KC * NB - 5, KC * NB - 1))


def step_mm(i):
    return START_MM + SLOT_MM * i


L_FRONT = 6
N_UNITS = GROUPS * (L_FRONT + 2) + 2 + 2 + 2 + KC + (GROUPS - 1) * 6 + 4 + KC + FFI * 6
W_O_PAIR = (N_UNITS - FFI * 6 - KC) // 2
JOBS_L = 4 * NB + 4 * NB + KC * NB
JOBS_A = KC * NB + 2 * NB + 2 * NB
KVG_DMAS = 16 * 7
JOBS_F = 2 * (4 * NB + KC * NB)


def build(nc, small_in, x_in, cs_in, w_in, kc_in, vc_in, y_out, kp_out, vp_out, ks_out, vs_out, tail_out):
    f32, f32r = mybir.dt.float32, mybir.dt.float32r
    ALU, ACT, AX = mybir.AluOpType, mybir.ActivationFunctionType, mybir.AxisListType

    kt_dram = nc.dram_tensor("kt_scratch", [KVH * HD, KW], f32, kind="Internal").ap()
    v_dram = nc.dram_tensor("v_scratch", [T, KVH * HD], f32, kind="Internal").ap()
    mb_dram = nc.dram_tensor("mb_scratch", [KC, P, T], f32, kind="Internal").ap()
    ta_dram = nc.dram_tensor("ta_scratch", [KC, P, T], f32, kind="Internal").ap()

    def blk(n):
        return slice(n * BW, (n + 1) * BW)

    ctx = ExitStack()
    with ctx:
        def tensor(stack, name, shape, dt=f32):
            return stack.enter_context(nc.sbuf_tensor(name, shape, dt))

        def sem(name):
            return ctx.enter_context(nc.semaphore(name))

        small = tensor(ctx, "small", [P, C_END])
        vt = tensor(ctx, "vt", [P, KC, NV])
        nsink = tensor(ctx, "nsink", [P, D // P])
        wraw = tensor(ctx, "wraw", [P, 2, UW])
        wh = tensor(ctx, "wh", [P, 2, UW], f32r)
        wl = tensor(ctx, "wl", [P, 2, UW], f32r)
        acc = tensor(ctx, "acc", [P, KC, T])
        acth = tensor(ctx, "acth", [P, KC, T], f32r)
        actl = tensor(ctx, "actl", [P, KC, T], f32r)
        ident = small[:, C_ID:C_ID + P]
        ones = small[:, C_ONE:C_ONE + P]
        blkones = small[:, C_BLK:C_BLK + P]
        perm = small[:, C_PERM:C_PERM + P]
        vec_in = small[:, C_VEC:C_GAIN].rearrange("p (c k) -> p c k", k=NV_IN)
        sink = small[:, C_SINK:C_END]

        with ExitStack() as s:
            xsq = tensor(s, "xsq", [P, NB, KC, BW])
            xstd = tensor(s, "xstd", [P, NB, BW])
            x32 = tensor(s, "x32", [P, 4, BW])
            spt = tensor(s, "spt", [P, 6, KC])
        with ExitStack() as s:
            vg = tensor(s, "vg", [P, 2, NV])
            xp = tensor(s, "xp", [P, 2, XPW])
            xc = tensor(s, "xc", [P, 2, T])
            ti = tensor(s, "ti", [P, 2, T])
            aa = tensor(s, "aa", [P, 2, T])
            gel = tensor(s, "gel", [P, 2, T])
            xch = tensor(s, "xch", [P, 2, T], f32r)
            xcl = tensor(s, "xcl", [P, 2, T], f32r)
            ph = tensor(s, "ph", [P, 2, T], f32r)
            pl = tensor(s, "pl", [P, 2, T], f32r)
            tail = tensor(s, "tail", [P, KC, 8])
            vst = tensor(s, "vst", [P, 2, KVH * HD])
        with ExitStack() as s:
            oh = tensor(s, "oh", [P, 2, T], f32r)
            ol = tensor(s, "ol", [P, 2, T], f32r)
            cs = tensor(s, "cs", [P, 2, T])
            qsb = tensor(s, "qsb", [P, 2, BW])
            qsq = tensor(s, "qsq", [P, 2, BW])
            qstd = tensor(s, "qstd", [P, 2, BW])
            rt1 = tensor(s, "rt1", [P, BW])
            rt2 = tensor(s, "rt2", [P, BW])
            kst = tensor(s, "kst", [P, 2, BW])
            kg = tensor(s, "kg", [P, 2, KW])
            vgr = tensor(s, "vgr", [P, AU, HD])
            qt = tensor(s, "qt", [P, 2 * T])
            tg = tensor(s, "tg", [P, 3, BW])
            pr = tensor(s, "pr", [P, 3, 2, P])
            pt = tensor(s, "pt", [P, 2, 2 * P])
            o32 = tensor(s, "o32", [P, 2, 2, CHUNK])
            snk = tensor(s, "snk", [P, 2, 2])
            sm = tensor(s, "sm", [P, 3, 6, 2])
        with ExitStack() as s:
            tensor(s, "hold", [P, 4, T])
            mg = tensor(s, "mg", [P, 5, 2, T])
        n2h = tensor(ctx, "n2h", [P, KC, T], f32r)
        n2l = tensor(ctx, "n2l", [P, KC, T], f32r)
        ssum = tensor(ctx, "ssum", [P, T])
        with ExitStack() as s:
            xr = tensor(s, "xr", [P, NB, BW])
            x1sq = tensor(s, "x1sq", [P, 2, BW])
        with ExitStack() as s:
            sg = tensor(s, "sg", [P, NB, BW])
            tu = tensor(s, "tu", [P, 2, BW])
        hh = acth[:, 0:4, :].rearrange("p (s c) t -> p s c t", s=2)
        hl = actl[:, 0:4, :].rearrange("p (s c) t -> p s c t", s=2)

        bank = [ctx.enter_context(nc.psum_tensor(f"bank{i}", [P, 512], f32)) for i in range(8)]
        aux0, aux1 = bank[6], bank[7]
        sbank = bank[RING_A:RING_A + 2]

        small_in_s, x_in_s = sem("small_loaded"), [sem(f"x_loaded{n}") for n in range(NB)]
        x_half_s = sem("x_loaded0_second_half")
        raw_loaded = [sem(f"weights_loaded{i}") for i in range(2)]
        split_done, unit_done, job_done = sem("weights_split"), sem("unit_done"), sem("job_done")
        free = [sem(f"bank_free{i}") for i in range(6)]
        vec_done, sp_act = sem("vectors_done"), sem("softplus_exp")
        xsq_done, xss_done, xstd_done, xrec_done = sem("x_squared"), sem("x_sumsq"), sem("x_std"), sem("x_rstd")
        x32_done, xh_done, xl_done, xlp_done = sem("x_normed"), sem("x_high"), sem("x_low"), sem("x_low_pool")
        zero_done, lru_zero_done = sem("sums_zeroed"), sem("lru_sums_zeroed")
        vg_done, pad_done, conv_done, tail_done = sem("lru_vectors"), sem("conv_pads"), sem("conv_taps"), sem("tails")
        xch_done, xcl_done, a_done, tau_done = sem("conv_high"), sem("conv_low"), sem("lru_a"), sem("lru_tau")
        ix_done, aa_done, msq_done, mult_done = sem("lru_gated_x"), sem("lru_a_squared"), sem("lru_mult_squared"), sem("lru_mult")
        one_done, b_done, h_done, prod_done = sem("lru_first_mult"), sem("lru_b"), sem("lru_h"), sem("lru_product")
        ph_done, pl_done = sem("product_high"), sem("product_low")
        v_stored, kv_stored, cs_loaded = [sem(f"v_stored{i}") for i in range(2)], sem("kv_stored"), sem("rope_loaded")
        ss_done, rot_done, std_done = sem("qk_sumsq"), sem("qk_rotated"), sem("qk_std")
        rot_used, t1_done, rsum_done, rrec_done, rope_done = (
            sem("rope_sin"), sem("rope_cos"), sem("rope_sum"), sem("qk_rstd"), sem("rope_done"))
        k_stored = [sem(f"k_stored{i}") for i in range(2)]
        gb_done, mb_stored = sem("lru_gated"), [sem(f"mb_stored{i}") for i in range(2)]
        kvg_loaded, kz_done = sem("kv_group_loaded"), sem("key_zeros")
        snk_done = sem("sinks_done")
        s_done, t_done, o_done = sem("scores_done"), sem("probs_transposed"), sem("attended")
        mx_done, nm0_done, nm_done = sem("row_max"), sem("neg_max"), sem("sink_less_max")
        exp_done, den_done, rc_done, p_done = sem("exp_done"), sem("denominator"), sem("denominator_inverse"), sem("probs_done")
        pt_done, o32_done, oh_done, ol_done = sem("probs_t_copied"), sem("o_copied"), sem("o_high"), sem("o_low")
        ta_stored = [sem(f"ta_stored{i}") for i in range(NB)]
        mg_loaded = [sem(f"merge_loaded{i}") for i in range(5)]
        mg1_done, mg2_done, mh_done, ml_done = sem("merge_a"), sem("merged"), sem("merged_high"), sem("merged_low")
        xr_loaded = [sem(f"x_again{n}") for n in range(NB)]
        n2h_done, x1sq_done, n2l_done, ssum_done = sem("n2_high"), sem("x1_squared"), sem("n2_low"), sem("x1_sumsq")
        ssall_done, std2_done, rstd2_done = sem("x1_sumsq_all"), sem("x1_std"), sem("x1_rstd")
        silu_done, h32_done, hh_done, hl_done = (
            sem("silu_done"), sem("hidden"), sem("hidden_high"), sem("hidden_low"))
        stored = sem("outputs_stored")
        block = ctx.enter_context(nc.Block())

        def wait(eng, s, value):
            if isinstance(value, int):
                if value > 0:
                    eng.wait_ge(s, value)
            else:
                v = eng.to_reg(value) if eng is nc.gpsimd else eng.snap(value)
                eng.wait_ge(small_in_s, 16)
                eng.wait_ge(s, v)

        @block.gpsimd
        def _(pool):
            def split(i, u, first):
                wait(pool, raw_loaded[u], 16 * i + 16)
                if not first:
                    wait(pool, unit_done, 2 * i + u - 1)
                for half in range(2):
                    c = slice(half * UW // 2, (half + 1) * UW // 2)
                    nc.gpsimd.tensor_scalar(wh[:, u, c], wraw[:, u, c], 1.0, 0.0, ALU.mult, ALU.add).then_inc(split_done, 1)
                    wait(pool, split_done, 8 * i + 4 * u + 2 * half + 1)
                    nc.gpsimd.tensor_tensor(wl[:, u, c], wraw[:, u, c], wh[:, u, c].bitcast(f32), ALU.subtract)\
                        .then_inc(split_done, 1)

            for u in range(2):
                split(0, u, True)
            for i in range(KC * NB):
                c, n = i % KC, i // KC
                if c % 4:
                    pool.wait_ge(xh_done, i + 1)
                    nc.gpsimd.tensor_tensor(actl[:, c, blk(n)], x32[:, c % 4, :], acth[:, c, blk(n)].bitcast(f32),
                                            ALU.subtract).then_inc(xlp_done, 1)
            def zero(half):
                nc.gpsimd.memset(acc[:, 4 * half:4 * half + 4, :], 0.0).then_inc(lru_zero_done, 1)

            split(1, 0, False)
            zero(0)
            split(1, 1, False)
            split(2, 0, False)
            zero(1)
            split(2, 1, False)
            with pool.Fori(3, W_O_PAIR) as i:
                for u in range(2):
                    split(i, u, False)

            def merge_low(m):
                pool.wait_ge(mh_done, m + 1)
                nc.gpsimd.tensor_tensor(actl[:, m, :], mg[:, m % 5, 0, :], acth[:, m, :].bitcast(f32), ALU.subtract)\
                    .then_inc(ml_done, 1)

            for m in range(KC):
                if m in (3, 6):
                    split(W_O_PAIR, m // 3 - 1, False)
                merge_low(m)
            with pool.Fori(W_O_PAIR + 1, N_UNITS // 2) as i:
                for u in range(2):
                    split(i, u, False)

        @block.tensor
        def _(pe):
            plan = Plan(job_done, unit_done)

            def mm(*args, **kw):
                return nc.tensor.matmul(*args, **kw)

            def weights(ahead=0, half=0):
                wait(pe, split_done, 4 * plan.units.value(ahead) + 2 * half + 2)

            def products(out, lhs, rhs, cols, first, last):
                mm(out, lhs[0], rhs[0][cols], start=first, stop=False)
                mm(out, lhs[0], rhs[1][cols], start=False, stop=False)
                return mm(out, lhs[1], rhs[0][cols], start=False, stop=last)

            def dense_block(slot, n, rh, rl, each=None, ahead=0, before=None):
                job = plan.take(last=n == NB - 1)
                wait(pe, free[job.bank], job.before)
                out = bank[job.bank][:, 0:BW]
                for k in range(KC):
                    if n == 0 and k % 4 == 0:
                        weights(ahead, k // 4)
                    if before:
                        before(n, k)
                    w = slice(k * P, (k + 1) * P)
                    for lhs, rhs in ((wh, rh), (wh, rl), (wl, rh)):
                        i = mm(out, lhs[:, slot, w], rhs[:, k, blk(n)], start=k == 0 and rhs is rh and lhs is wh,
                               stop=k == KC - 1 and lhs is wl)
                        if k == KC - 1 and lhs is wl:
                            i.then_inc(job.done[0], 1)
                        if each:
                            each()
                return job

            def dense(slot, rh, rl, each=None):
                for n in range(NB):
                    dense_block(slot, n, rh, rl, each)

            def down(rh, rl):
                for half in range(2):
                    for ml in range(4):
                        if ml % 2 == 0:
                            weights(0, ml // 2)
                        for n in range(NB):
                            job = plan.take(last=ml == 3 and n == NB - 1)
                            wait(pe, free[job.bank], job.before)
                            out = bank[job.bank][:, 0:BW]
                            for k in range(2):
                                w = slice((2 * ml + k) * P, (2 * ml + k + 1) * P)
                                mm(out, wh[:, half, w], rh[:, k, blk(n)], start=k == 0, stop=False)
                                mm(out, wh[:, half, w], rl[:, k, blk(n)], start=False, stop=False)
                                i3 = mm(out, wl[:, half, w], rh[:, k, blk(n)], start=False, stop=k == 1)
                            i3.then_inc(job.done[0], 1)

            pe.wait_ge(small_in_s, 16)
            def sumsq(n):
                if n == 2:
                    pe.wait_ge(xstd_done, 1)
                for c in range(KC):
                    if c % 4 == 0:
                        pe.wait_ge(xsq_done, 2 * n + c // 4 + 1)
                    i = mm((aux0, aux1)[n % 2][:, 0:BW], ones, xsq[:, n, c, :], start=c == 0, stop=c == KC - 1)
                i.then_inc(xss_done, 1)

            sumsq(0)
            sumsq(1)

            def lru_front(g, first):
                if first:
                    for n in range(NB):
                        pe.wait_ge(xl_done, KC // 4 * (n + 1))
                        pe.wait_ge(xlp_done, 3 * KC // 4 * (n + 1))
                        for i in range(2):
                            dense_block(i, n, acth, actl, ahead=i)
                            if n == 0 and i == 0:
                                sumsq(2)
                else:
                    for i in range(2):
                        dense(i, acth, actl)
                for i in range(2):
                    dense(0, acth, actl)
                    weights()
                    wait(pe, xcl_done, 2 * g + i + 1)
                    for gate in range(2):
                        for n in range(NB):
                            job = plan.take(last=gate == 1 and n == NB - 1)
                            wait(pe, free[job.bank], job.before)
                            out, w = bank[job.bank][:, 0:BW], slice(gate * P, (gate + 1) * P)
                            mm(out, wh[:, 1, w], xch[:, i, blk(n)], start=True, stop=False)
                            mm(out, wh[:, 1, w], xcl[:, i, blk(n)], start=False, stop=False)
                            mm(out, wl[:, 1, w], xch[:, i, blk(n)], start=False, stop=True).then_inc(job.done[0], 1)

            def lru_down(g):
                wait(pe, pl_done, 2 * g + 2)
                down(ph, pl)

            lru_front(0, True)
            with pe.Fori(1, GROUPS) as g:
                plan.loop(g, 1, JOBS_L, L_FRONT + 2)
                lru_front(g, False)
                lru_down(g - 1)
            plan.end(GROUPS - 1)

            for t in range(9):
                if t == 8:
                    plan.units.add()
                job = plan.take(last=t == 8)
                wait(pe, free[job.bank], job.before)
                out, c0 = bank[job.bank][:, 0:KVH * HD], min(t * P, T - P)
                for k in range(KC):
                    if t == 0 and k % 2 == 0:
                        weights(k // 4, k % 4 // 2)
                    w, x = slice(k % 4 * 256, k % 4 * 256 + 256), slice(c0, c0 + P)
                    mm(out, acth[:, k, x], wh[:, k // 4, w], start=k == 0, stop=False)
                    mm(out, acth[:, k, x], wl[:, k // 4, w], start=False, stop=False)
                    i = mm(out, actl[:, k, x], wh[:, k // 4, w], start=False, stop=k == KC - 1)
                    if t == 8 and k == 3:
                        i.then_inc(unit_done, 1)
                i.then_inc(job.done[0], 1)
            lru_down(GROUPS - 1)

            def qk_aux(base, k, b, after):
                wait(pe, free[b], after)
                wait(pe, std_done, base + k)
                mm(aux0[:, 0:BW], blkones, qsq[:, k % 2, :], start=True, stop=True).then_inc(ss_done, 1)
                wait(pe, rot_used, base + k)
                mm(aux1[:, 0:BW], perm, qsb[:, k % 2, :], start=True, stop=True).then_inc(rot_done, 1)

            def qk(base, late=None, attended=None):
                for i in range(2):
                    for n in range(NB):
                        job = dense_block(i, n, acth, actl)
                        if attended is not None and i == 0 and n == 1:
                            wait(pe, pt_done, attended)
                            wait(pe, o32_done, attended)
                        if late:
                            qk_aux(*late)
                        late = (base, NB * i + n, job.bank, job.after)
                return late

            late = qk(0)
            late = qk(6, late)

            for m in range(KC - 2):
                dense(m % 2, acth, actl)
                if m == 0:
                    qk_aux(*late)

            def attention_step(g, i):
                n0 = g * AU
                def probs():
                    wait(pe, p_done, n0 + i - 1)

                def probs_t():
                    wait(pe, pt_done, n0 + i - 2)
                    if i >= 4:
                        wait(pe, o32_done, n0 + i - 3)

                if i >= AU or i == 3:
                    probs_t()
                if i in (2, AU + 1):
                    probs()
                if i < AU:
                    if i >= 2:
                        wait(pe, exp_done, n0 + i - 1)
                    q, k, q0 = unit_shape(i)
                    k0 = q0 + q - k if i < AU - 1 else SEQ
                    mm(sbank[i % 2][0:2 * q, 0:2 * P].rearrange("p (h k) -> p h k", h=2)[:, :, 0:k],
                       qt[:, 2 * q0:2 * (q0 + q)], kg[:, :, k0:k0 + k], start=True, stop=True).then_inc(s_done, 1)
                if 0 <= i - 3 < AU:
                    q, k, _ = unit_shape(i - 3)
                    if 3 < i < AU:
                        probs_t()
                    for h in range(2):
                        x = mm(aux0[h * HD:(h + 1) * HD, 0:2 * q], vgr[0:k, i - 3, :],
                               pt[0:k, (i - 3) % 2, h * 2 * q:(h + 1) * 2 * q], start=True, stop=True)
                    x.then_inc(o_done, 1)
                if 2 < i < AU + 1:
                    probs()
                if 0 <= i - 2 < AU:
                    q, k, _ = unit_shape(i - 2)
                    for h in range(2):
                        x = nc.tensor.transpose(aux1[0:k, h * 2 * q:(h + 1) * 2 * q], pr[0:2 * q, (i - 2) % 3, h, 0:k],
                                                ident[0:2 * q, 0:2 * q])
                    x.then_inc(t_done, 1)

            def down_blocks(slot, rh, rl, each):
                for n in range(NB):
                    for m in range(KC):
                        if n == 0 and m % 2 == 0:
                            weights(m // 4, m % 4 // 2)
                        job = side_down(plan, n * KC + m)
                        wait(pe, free[job.bank], job.before)
                        out = bank[job.bank][:, 0:BW]
                        for k in range(2):
                            w = slice((2 * (m % 4) + k) * P, (2 * (m % 4) + k + 1) * P)
                            u = (slot + m // 4) % 2
                            mm(out, wh[:, u, w], rh[:, k, blk(n)], start=k == 0, stop=False)
                            each()
                            mm(out, wh[:, u, w], rl[:, k, blk(n)], start=False, stop=False)
                            each()
                            i3 = mm(out, wl[:, u, w], rh[:, k, blk(n)], start=False, stop=k == 1)
                            if k == 1:
                                i3.then_inc(job.done[0], 1)
                            each()

            def group(g, first, last):
                done = [0, 0]
                b = (plan.bank - 1) % RING_A
                late = (6 * g + 6, 5, b, plan.uses[b].value())

                def each():
                    done[0] += 1
                    if done[0] == 9 and not first:
                        qk_aux(*late)
                    if done[1] < ASLOTS and done[0] == step_mm(done[1]):
                        if done[1] == 0:
                            wait(pe, rope_done, 6 * g + 12)
                            wait(pe, kvg_loaded, KVG_DMAS * (g + 1))
                            wait(pe, kz_done, 2)
                        attention_step(g, done[1])
                        done[1] += 1

                dense(0, acth, actl, each)
                if first:
                    for i in range(2):
                        dense(1 - i, acth, actl, each)
                else:
                    wait(pe, ol_done, AU * g)
                    down_blocks(1, oh, ol, each)
                dense(1, acth, actl, each)
                assert done[1] == ASLOTS and done[0] == SIDE_MM
                if last:
                    plan.ring(6)
                    wait(pe, ol_done, AU * (g + 1))
                    down(oh, ol)
                else:
                    qk(6 * g + 12, attended=AU * (g + 1))

            for b in (RING_A, RING_A + 1):
                pe.wait_ge(free[b], plan.uses[b].value())
            plan.ring(RING_A)
            group(0, True, False)
            with pe.Fori(1, GROUPS - 1) as g:
                plan.loop(g, 1, JOBS_A, 6)
                group(g, False, False)
            plan.end(GROUPS - 2)
            group(GROUPS - 1, False, True)

            jobs = [plan.take(last=j % NB == NB - 1) for j in range(2 * NB)]
            units = plan.units.value() - 2
            for slot, chunks in ((0, range(0, 6)), (1, range(0, 6)), (0, range(6, KC)), (1, range(6, KC))):
                for k in chunks:
                    pe.wait_ge(split_done, 4 * (units + slot) + 2 * (k // 4) + 2)
                    pe.wait_ge(ml_done, k + 1)
                    w = slice(k * P, (k + 1) * P)
                    for n in range(NB):
                        job = jobs[slot * NB + n]
                        if k == 0:
                            pe.wait_ge(free[job.bank], job.before)
                        out = bank[job.bank][:, 0:BW]
                        mm(out, wh[:, slot, w], acth[:, k, blk(n)], start=k == 0, stop=False)
                        mm(out, wh[:, slot, w], actl[:, k, blk(n)], start=False, stop=False)
                        i3 = mm(out, wl[:, slot, w], acth[:, k, blk(n)], start=False, stop=k == KC - 1)
                        if k == KC - 1:
                            i3.then_inc(job.done[0], 1)
            with pe.Fori(1, KC // 2) as i:
                plan.loop(i, 1, 2 * NB, 2)
                for slot in range(2):
                    dense(slot, acth, actl)
            plan.end(KC // 2 - 1)

            def sumsq2():
                for n in range(NB):
                    if n == 2:
                        pe.wait_ge(std2_done, 1)
                    mm((aux0, aux1)[n % 2][:, 0:BW], ones, ssum[:, blk(n)], start=True, stop=True).then_inc(ssall_done, 1)

            def x1_ready(n, k):
                pe.wait_ge(n2l_done, NB * k + n + 1)

            def ffn_front(first):
                for i in range(4):
                    for n in range(NB):
                        dense_block(i % 2, n, n2h, n2l, before=x1_ready if first and i == 0 else None)
                    if first and i == 0:
                        pe.wait_ge(ssum_done, KC * NB)
                        sumsq2()

            def ffn_down(i, slot):
                wait(pe, hl_done, 6 * i + 6)
                down(hh[:, slot], hl[:, slot])

            ffn_front(True)
            with pe.Fori(0, FFI // 2) as j:
                plan.loop(j, 0, JOBS_F, 12)
                for s in range(2):
                    ffn_front(False)
                    ffn_down(2 * j + s, s)
            plan.end(FFI // 2)
            ffn_down(FFI - 1, 0)
            assert plan.units.value() == N_UNITS and (N_UNITS - FFI * 6 - KC) % 2 == 0

        @block.scalar
        def _(act):
            plan = Plan(job_done, unit_done)
            f = nc.scalar.activation

            act.dma_start(kt_dram[:, SEQ:SEQ + KV_CACHED], kc_in[:, WINDOW - KV_CACHED:WINDOW]).then_inc(kv_stored, 16)
            act.dma_start(ks_out[:, 0:WINDOW - DEC], kc_in[:, DEC:WINDOW]).then_inc(kv_stored, 16)
            act.dma_start(vs_out[0:WINDOW - DEC, :], vc_in[DEC:WINDOW, :]).then_inc(kv_stored, 16)

            act.wait_ge(small_in_s, 16)
            f(spt[:, 0, :], vec_in[:, :, V_LAM], ACT.Abs).then_inc(sp_act, 1)
            act.wait_ge(sp_act, 1)
            f(spt[:, 1, :], spt[:, 0, :], ACT.Exp, scale=-1.0).then_inc(sp_act, 1)
            def squares(n):
                act.wait_ge(x_in_s[n], 16)
                for half in range(2):
                    if n == 0 and half == 1:
                        act.wait_ge(x_half_s, 16)
                    cs4 = slice(4 * half, 4 * half + 4)
                    f(xsq[:, n, cs4, :], acc[:, cs4, blk(n)], ACT.Square).then_inc(xsq_done, 1)

            def root(n):
                act.wait_ge(xss_done, n + 1)
                f(xstd[:, n, :], (aux0, aux1)[n % 2][:, 0:BW], ACT.Sqrt, scale=1.0 / D, bias=EPS).then_inc(xstd_done, 1)

            def high(n, chunks):
                for c in chunks:
                    act.wait_ge(x32_done, n * KC + c + 1)
                    f(acth[:, c, blk(n)], x32[:, c % 4, :], ACT.Copy).then_inc(xh_done, 1)

            squares(0)
            root(0)
            squares(1)
            high(0, range(0, 6))
            root(1)
            high(0, range(6, KC))
            squares(2)
            high(1, range(KC))
            root(2)
            high(2, range(KC))

            def blocks(by_block):
                return [(i, n) for n in range(NB) for i in range(2)] if by_block else [(i, n) for i in range(2) for n in range(NB)]

            def lru_front(g, first):
                for i, n in blocks(first):
                    if n == 0:
                        if not first:
                            wait(act, msq_done, 2 * g + i - 1)
                        elif i == 0:
                            act.wait_ge(xl_done, KC * NB // 4)
                            act.wait_ge(xlp_done, 3 * KC * NB // 4)
                    job = plan.take(last=n == NB - 1)
                    wait(act, *job.done)
                    ps, c0 = bank[job.bank], CONV - 1 + n * BW
                    if n < NB - 1:
                        f(xp[:, i, c0:c0 + BW], ps[:, 0:BW], ACT.Copy).then_inc(free[job.bank], 1)
                    else:
                        f(xp[:, i, c0:SX0], ps[:, 0:BW - DEC], ACT.Copy)
                        f(xp[:, i, SX1:XPW], ps[:, BW - DEC:BW], ACT.Copy).then_inc(free[job.bank], 1)

                def conv_high(i):
                    wait(act, conv_done, 16 * g + 8 * i + 8)
                    f(xch[:, i, :], xc[:, i, :], ACT.Copy).then_inc(xch_done, 1)

                conv_high(0)
                wait(act, vg_done, g + 1)
                for i in range(2):
                    if not first:
                        wait(act, pl_done, 2 * g + i - 1)
                    for n in range(NB):
                        job = plan.take(last=n == NB - 1)
                        wait(act, *job.done)
                        f(gel[:, i, blk(n)], bank[job.bank][:, 0:BW], ACT.Gelu_apprx_tanh).then_inc(free[job.bank], 1)
                    wait(act, xcl_done, 2 * g + i + 1)
                    for gate in range(2):
                        for n in range(NB):
                            job = plan.take(last=gate == 1 and n == NB - 1)
                            wait(act, *job.done)
                            dst = (xp, ti)[gate][:, i, blk(n)]
                            f(dst, bank[job.bank][:, 0:BW], ACT.Tanh, scale=0.5,
                              bias=vg[:, i, V_BR + gate:V_BR + gate + 1]).then_inc(free[job.bank], 1)
                    if i == 0:
                        conv_high(1)
                for i in range(2):
                    if i == 0:
                        wait(act, free[job.bank], job.after)
                    f(aa[:, i, :], xp[:, i, 0:T], ACT.Exp, scale=vg[:, i, V_NSP:V_NSP + 1],
                      bias=vg[:, i, V_NSP:V_NSP + 1]).then_inc(a_done, 1)
                    wait(act, a_done, 2 * g + i + 1)
                    f(xp[:, i, 0:T], xp[:, i, 0:T], ACT.Tanh, scale=vg[:, i, V_SP:V_SP + 1],
                      bias=vg[:, i, V_SP:V_SP + 1]).then_inc(tau_done, 1)
                    wait(act, ix_done, 2 * g + i + 1)
                    f(xc[:, i, :], aa[:, i, :], ACT.Square).then_inc(aa_done, 1)
                for i in range(2):
                    wait(act, msq_done, 2 * g + i + 1)
                    f(xc[:, i, :], xc[:, i, :], ACT.Sqrt).then_inc(mult_done, 1)

            def lru_products(g):
                for i in range(2):
                    wait(act, prod_done, 2 * g + i + 1)
                    if i == 0:
                        wait(act, unit_done, plan.units.value())
                    f(ph[:, i, :], gel[:, i, :], ACT.Copy).then_inc(ph_done, 1)

            def skip_down():
                for k in range(2 * 4 * NB):
                    plan.take(last=k % (4 * NB) == 4 * NB - 1)

            lru_front(0, True)
            lru_products(0)
            with act.Fori(1, GROUPS) as g:
                plan.loop(g, 1, JOBS_L, L_FRONT + 2)
                lru_front(g, False)
                skip_down()
                lru_products(g)
            plan.end(GROUPS - 1)

            def store_v(t):
                act.wait_ge(free[vjobs[t].bank], vjobs[t].after)
                if t < 8:
                    act.dma_start(v_dram[t * P:(t + 1) * P, :], vst[:, t % 2, :]).then_inc(v_stored[t % 2], 16)
                else:
                    act.dma_start(v_dram[SEQ:T, :], vst[P - DEC:P, t % 2, :]).then_inc(v_stored[0], 16)
                    act.dma_start(vs_out[WINDOW - DEC:WINDOW, :], vst[P - DEC:P, 0, :]).then_inc(stored, 16)
                if t == 7:
                    act.dma_start(vp_out[:, :], vst[:, 1, :]).then_inc(stored, 16)

            vjobs = []
            for t in range(9):
                if t == 8:
                    plan.units.add()
                job = plan.take(last=t == 8)
                vjobs.append(job)
                act.wait_ge(*job.done)
                if t >= 2:
                    act.wait_ge(v_stored[t % 2], 16 * (t // 2))
                f(vst[:, t % 2, :], bank[job.bank][:, 0:KVH * HD], ACT.Copy).then_inc(free[job.bank], 1)
                if t >= 1:
                    store_v(t - 1)
            store_v(8)
            skip_down()
            act.wait_ge(tail_done, 6 * GROUPS)
            act.dma_start(tail_out, tail[:, :, :]).then_inc(stored, 16)
            act.wait_ge(unit_done, plan.units.value())
            act.wait_ge(v_stored[0], 16 * 5)
            act.wait_ge(v_stored[1], 16 * 4)
            act.wait_ge(stored, 16 * 3)
            act.dma_start(cs[:, :, :], cs_in).then_inc(cs_loaded, 16)

            def qk_copy(base, k, gain):
                job = plan.take(last=k % NB == NB - 1)
                wait(act, *job.done)
                wait(act, rot_done, base + k - 1)
                wait(act, t1_done, base + k - 1)
                f(qsq[:, k % 2, :], bank[job.bank][:, 0:BW], ACT.Square)
                f(qsb[:, k % 2, :], bank[job.bank][:, 0:BW], ACT.Identity, scale=gain).then_inc(free[job.bank], 1)

            def qk_root(base, k):
                wait(act, ss_done, base + k + 1)
                wait(act, rope_done, base + k - 1)
                f(qstd[:, k % 2, :], aux0[:, 0:BW], ACT.Sqrt, scale=1.0 / HD, bias=EPS).then_inc(std_done, 1)

            def store_k(k):
                act.wait_ge(rope_done, k + 1)
                n, slot, rows = k % NB, k % 2, slice(k // NB * P, (k // NB + 1) * P)
                if n < NB - 1:
                    act.dma_start(kt_dram[rows, blk(n)], kst[:, slot, :]).then_inc(k_stored[slot], 16)
                else:
                    a = SEQ - n * BW
                    act.dma_start(kt_dram[rows, n * BW:SEQ], kst[:, slot, 0:a]).then_inc(k_stored[slot], 16)
                    act.dma_start(kt_dram[rows, SEQ + KV_CACHED:KW], kst[:, slot, a:BW]).then_inc(k_stored[slot], 16)
                    act.dma_start(kp_out[rows, :], kst[:, slot, a - WINDOW:a]).then_inc(k_stored[slot], 16)
                    act.dma_start(ks_out[rows, WINDOW - DEC:WINDOW], kst[:, slot, a:BW]).then_inc(k_stored[slot], 16)

            qgain, kgain = small[:, C_GAIN:C_GAIN + 1], small[:, C_GAIN + 1:C_GAIN + 2]
            for k in range(6):
                qk_copy(0, k, kgain)
                if k >= 1:
                    qk_root(0, k - 1)
                if k >= 2:
                    store_k(k - 2)
            for k in range(6):
                qk_copy(6, k, qgain)
                if k == 0:
                    qk_root(0, 5)
                else:
                    qk_root(6, k - 1)
                if k < 2:
                    store_k(4 + k)

            def load_group(g, part):
                cols = bass.ds(g * HD, HD)
                lower = v_dram[0:SEQ - CHUNK, cols].rearrange("(u p) d -> p u d", p=CHUNK)
                upper = v_dram[CHUNK:SEQ, cols].rearrange("(u p) d -> p u d", p=CHUNK)
                for dst, src in [(kg[0:HD, 0, :], kt_dram[cols, :]),
                                 (kg[HD:P, 1, :], kt_dram[cols, :]),
                                 (vgr[0:CHUNK, 1:AU - 1, :], lower),
                                 (vgr[CHUNK:P, 1:AU - 1, :], upper),
                                 (vgr[0:CHUNK, 0, :], v_dram[0:CHUNK, cols]),
                                 (vgr[0:KV_CACHED, AU - 1, :], vc_in[WINDOW - KV_CACHED:WINDOW, cols]),
                                 (vgr[KV_CACHED:KV_CACHED + DEC, AU - 1, :], v_dram[SEQ:T, cols])][part]:
                    act.dma_start(dst, src).then_inc(kvg_loaded, 16)

            def store_mb(m):
                act.wait_ge(gb_done, NB * (m + 1))
                act.dma_start(mb_dram[m], acc[:, m, :]).then_inc(mb_stored[m // 4], 16)

            def gate_b(m, n):
                job = plan.take(last=n == NB - 1)
                act.wait_ge(*job.done)
                wait(act, gb_done, NB * (m - 1) + n + 1)
                f(tg[:, n, :], bank[job.bank][:, 0:BW], ACT.Tanh, scale=0.5).then_inc(free[job.bank], 1)
                if m == 0 and n == 0:
                    qk_root(6, 5)
                if m >= 1 and n == 1:
                    store_mb(m - 1)

            for m in range(KC - 2):
                for n in range(NB):
                    gate_b(m, n)
                if m == 0:
                    act.wait_ge(k_stored[0], 16 * 6)
                    act.wait_ge(k_stored[1], 16 * 6)
                    act.wait_ge(kv_stored, 16 * 3)
                    load_group(0, slice(0, 7))

            def attention_step(g, i, read):
                n0 = g * AU
                if 0 <= i - 2 < AU:
                    q, k, _ = unit_shape(i - 2)
                    wait(act, t_done, n0 + i - 1)
                    if i >= 3:
                        wait(act, o_done, n0 + i - 3)
                    f(pt[0:k, i % 2, 0:4 * q], aux1[0:k, 0:4 * q], ACT.Copy).then_inc(pt_done, 1)
                if 0 <= i - 4 < AU:
                    q, _, q0 = unit_shape(i - 4)
                    if i - 4 in read:
                        wait(act, *read[i - 4])
                    wait(act, o32_done, n0 + i - 3)
                    f(oh[:, :, q0:q0 + q], o32[:, i % 2, :, 0:q], ACT.Copy).then_inc(oh_done, 1)
                if i < AU:
                    q, k, _ = unit_shape(i)
                    r = i % 3
                    wait(act, nm_done, n0 + i + 1)
                    if i >= 3:
                        wait(act, t_done, n0 + i - 2)
                    for h in range(2):
                        f(pr[0:2 * q, r, h, 0:k], sbank[i % 2][0:2 * q, h * P:h * P + k], ACT.Exp, scale=HD ** -0.5,
                          bias=sm[0:2 * q, r, 1, h:h + 1], accum_out=sm[0:2 * q, r, 3, h:h + 1])
                    f(sm[0:2 * q, r, 4, :], sm[0:2 * q, r, 2, :], ACT.Exp).then_inc(exp_done, 1)

            def group(g, first, last):
                jobs, read = [], {}
                if not first:
                    qk_root(6 * g + 6, 5)

                def skip_down_blocks():
                    down = [side_down(plan, k) for k in range(KC * NB)]
                    for n in range(NB):
                        read[n * BW // CHUNK] = down[(n + 1) * KC - 1].done

                def store_ta(j):
                    wait(act, free[jobs[j].bank], jobs[j].after)
                    act.dma_start(ta_dram[2 * g + j // NB, :, blk(j % NB)], tg[:, j % NB, :])\
                        .then_inc(ta_stored[j % NB], 16)

                def gate_a(j):
                    job = plan.take(last=j % NB == NB - 1)
                    jobs.append(job)
                    wait(act, *job.done)
                    if j >= NB:
                        wait(act, ta_stored[j % NB], 32 * g + 16)
                    elif first:
                        wait(act, gb_done, NB * (KC - 1) + j + 1)
                    f(tg[:, j % NB, :], bank[job.bank][:, 0:BW], ACT.Tanh, scale=0.5).then_inc(free[job.bank], 1)
                    if j == 0 and first:
                        store_mb(KC - 1)
                    if j >= 1:
                        store_ta(j - 1)

                def side_job(j):
                    if first and j < 2 * NB:
                        gate_b(KC - 2 + j // NB, j % NB)
                    else:
                        gate_a(j - 2 * NB if first else j)
                    if not first and j == NB - 1:
                        skip_down_blocks()

                def side_end(j):
                    return 3 * KC * (j + 1) + (6 * KC * NB if not first and j >= NB else 0)

                j = 0
                for i in range(ASLOTS + 2):
                    while j < (4 if first else 2) * NB and (i >= ASLOTS or side_end(j) <= step_mm(i)):
                        side_job(j)
                        j += 1
                    attention_step(g, i, read)
                    if last and i == 1:
                        act.wait_ge(rope_done, 6 * GROUPS + 6)
                        for half in range(2):
                            act.wait_ge(mb_stored[half], 16 * KC // 2)
                        for n in range(NB):
                            act.wait_ge(ta_stored[n], 32 * g)
                        for m in range(2):
                            load_merge(m)
                store_ta(2 * NB - 1)
                if not last:
                    for k in range(6):
                        qk_copy(6 * g + 12, k, qgain)
                        load_group(g + 1, slice(2 * k, 2 * k + 2))
                        if k >= 1:
                            qk_root(6 * g + 12, k - 1)
                    for n in range(NB):
                        wait(act, ta_stored[n], 32 * g + 32)

            def load_merge(m):
                act.dma_start(mg[:, m % 5, 0, :], ta_dram[m]).then_inc(mg_loaded[m % 5], 16)
                act.dma_start(mg[:, m % 5, 1, :], mb_dram[m]).then_inc(mg_loaded[m % 5], 16)

            plan.ring(RING_A)
            group(0, True, False)
            with act.Fori(1, GROUPS - 1) as g:
                plan.loop(g, 1, JOBS_A, 6)
                group(g, False, False)
            plan.end(GROUPS - 2)
            group(GROUPS - 1, False, True)
            plan.ring(6)
            skip_down()

            for n in range(NB):
                act.wait_ge(ta_stored[n], 16 * KC)
            act.wait_ge(ol_done, AU * GROUPS)
            for m in range(2, 5):
                load_merge(m)
            for n in range(NB):
                act.dma_start(xr[:, n, :], x_in[:, 0, blk(n)]).then_inc(xr_loaded[n], 16)
            for m in range(KC):
                act.wait_ge(mg2_done, m + 1)
                f(acth[:, m, :], mg[:, m % 5, 0, :], ACT.Copy).then_inc(mh_done, 1)
                if 1 <= m <= KC - 5:
                    act.wait_ge(ml_done, m)
                    load_merge(m + 4)

            def x1_parts(m, s, more):
                for n in range(NB):
                    job = plan.take(last=n == NB - 1)
                    wait(act, free[job.bank], job.after)
                    if more:
                        act.dma_start(xr[:, n, :], x_in[:, m + 1, blk(n)]).then_inc(xr_loaded[n], 16)
                    f(n2h[:, m, blk(n)], acc[:, m, blk(n)], ACT.Identity, scale=vt[:, m, V_G2:V_G2 + 1])\
                        .then_inc(n2h_done, 1)
                    f(x1sq[:, (s + n) % 2, :], acc[:, m, blk(n)], ACT.Square).then_inc(x1sq_done, 1)

            with act.Fori(0, KC // 2 - 1) as i:
                plan.loop(i, 0, 2 * NB, 2)
                for s in range(2):
                    x1_parts(2 * i + s, s, True)
            plan.end(KC // 2 - 1)
            for s in range(2):
                x1_parts(KC - 2 + s, s, s == 0)
            for n in range(NB):
                act.wait_ge(ssall_done, n + 1)
                f(ssum[:, blk(n)], (aux0, aux1)[n % 2][:, 0:BW], ACT.Sqrt, scale=1.0 / D, bias=EPS).then_inc(std2_done, 1)

            def ffn_front(i, slot):
                for c in range(2):
                    for n in range(NB):
                        job = plan.take(last=n == NB - 1)
                        wait(act, free[job.bank], job.after)
                        f(sg[:, n, :], sg[:, n, :], ACT.Silu).then_inc(silu_done, 1)
                    for n in range(NB):
                        plan.take(last=n == NB - 1)
                        wait(act, h32_done, 6 * i + NB * c + n + 1)
                        f(hh[:, slot, c, blk(n)], tu[:, (c + n) % 2, :], ACT.Copy).then_inc(hh_done, 1)

            ffn_front(0, 0)
            with act.Fori(0, FFI // 2) as j:
                plan.loop(j, 0, JOBS_F, 12)
                for s in range(2):
                    ffn_front(2 * j + 1 + s, 1 - s)
                    skip_down()
            plan.end(FFI // 2)

        final_jobs = []

        @block.vector
        def _(dve):
            plan = Plan(job_done, unit_done)
            V = nc.vector
            stt = V.scalar_tensor_tensor

            steps = [0]

            def vec(ins):
                ins.then_inc(vec_done, 1)
                steps[0] += 1
                dve.wait_ge(vec_done, steps[0])

            dve.wait_ge(small_in_s, 16)
            vec(V.tensor_copy(vt[:, :, 0:NV_IN], vec_in))
            vec(V.tensor_scalar(vt[:, :, V_BR:V_BI + 1], vec_in[:, :, V_BR:V_BI + 1], 0.5, None, ALU.mult))
            vec(V.tensor_scalar(nsink[:, :], sink, -1.0, None, ALU.mult))
            dve.wait_ge(sp_act, 2)
            e1, s1, s2, q1 = spt[:, 1, :], spt[:, 2, :], spt[:, 3, :], spt[:, 4, :]
            vec(V.tensor_scalar(s2, e1, 2.0, None, ALU.add))
            vec(V.reciprocal(q1, s2))
            vec(V.tensor_tensor(s1, e1, q1, ALU.mult))
            vec(V.tensor_tensor(s2, s1, s1, ALU.mult))
            vec(V.tensor_scalar(q1, s2, 1.0 / 15, None, ALU.mult))
            for n in (13, 11, 9, 7, 5, 3):
                vec(stt(q1, q1, 1.0 / n, s2, ALU.add, ALU.mult))
            vec(stt(q1, q1, 1.0, s1, ALU.add, ALU.mult))
            vec(V.tensor_scalar(s1, vec_in[:, :, V_LAM], -1.0, 0.0, ALU.mult, ALU.max))
            vec(stt(s1, q1, 2.0, s1, ALU.mult, ALU.add))
            vec(V.tensor_scalar(vt[:, :, V_SP], s1, 4.0, None, ALU.mult))
            vec(V.tensor_scalar(vt[:, :, V_NSP], s1, -4.0, None, ALU.mult))

            def x_low(i):
                dve.wait_ge(xh_done, i + 1)
                c, n = i % KC, i // KC
                V.tensor_tensor(actl[:, c, blk(n)], x32[:, c % 4, :], acth[:, c, blk(n)].bitcast(f32), ALU.subtract)\
                    .then_inc(xl_done, 1)

            for n in range(NB):
                dve.wait_ge(xstd_done, n + 1)
                V.reciprocal(xstd[:, n, :], xstd[:, n, :]).then_inc(xrec_done, 1)
                dve.wait_ge(xrec_done, n + 1)
                for c in range(KC):
                    i = n * KC + c
                    if c % 4:
                        wait(dve, xlp_done, 3 * (i // 4 - 1) + c % 4)
                    else:
                        wait(dve, xl_done, i // 4)
                    stt(x32[:, c % 4, :], acc[:, c, blk(n)], vt[:, c, V_G1:V_G1 + 1], xstd[:, n, :],
                        ALU.mult, ALU.mult).then_inc(x32_done, 1)
                    if c % 4 == 1:
                        x_low(i - 1)

            def skip(jobs, per_unit=NB):
                for n in range(jobs):
                    plan.take(last=n % per_unit == per_unit - 1)

            def add_down(half, ms=range(4)):
                for ml in ms:
                    for n in range(NB):
                        job = plan.take(last=ml == 3 and n == NB - 1)
                        wait(dve, *job.done)
                        a = acc[:, 4 * half + ml, blk(n)]
                        V.tensor_tensor(a, bank[job.bank][:, 0:BW], a, ALU.add).then_inc(free[job.bank], 1)
                return job

            def streams(i, j, src):
                return ((src[:, i, 0:SEQ], xp[:, i, j:j + SEQ]),
                        (src[:, i, SEQ:T], xp[:, i, SX0 + j:SX0 + j + DEC]))

            def lru_front(g, first):
                wait(dve, tau_done, 2 * g)
                V.tensor_copy(vg[:, :, :], vt[:, bass.ds(2 * g, 2), :]).then_inc(vg_done, 1)
                wait(dve, vg_done, g + 1)
                for i in range(2):
                    if not first:
                        wait(dve, msq_done, 2 * g + i - 1)
                    V.memset(xp[:, i, 0:CONV - 1], 0.0).then_inc(pad_done, 1)
                    V.tensor_copy(xp[:, i, SX0:SX1], vg[:, i, V_S0:V_S2 + 1]).then_inc(pad_done, 1)
                for i, n in [(i, n) for n in range(NB) for i in range(2)] if first else [(i, n) for i in range(2) for n in range(NB)]:
                    jobs[i] = plan.take(last=n == NB - 1)
                for i in range(2):
                    wait(dve, free[jobs[i].bank], jobs[i].after)
                    wait(dve, pad_done, 4 * g + 2 * i + 2)
                    if not first:
                        wait(dve, pl_done, 2 * g + i - 1)
                    c0 = 16 * g + 8 * i
                    for j in range(CONV):
                        w = vg[:, i, V_W0 + j:V_W0 + j + 1]
                        for s, (dst, src) in enumerate(streams(i, j, xc)):
                            if j == 0:
                                V.tensor_scalar(dst, src, w, vg[:, i, V_CB:V_CB + 1], ALU.mult, ALU.add).then_inc(conv_done, 1)
                            else:
                                wait(dve, conv_done, c0 + 2 * j - 1 + s)
                                stt(dst, src, w, dst, ALU.mult, ALU.add).then_inc(conv_done, 1)
                    c = 2 * g + i
                    V.tensor_copy(tail[:, c, 0:3], xp[:, i, SEQ:SX0]).then_inc(tail_done, 1)
                    V.tensor_copy(tail[:, c, 3:6], xp[:, i, XPW - 3:XPW]).then_inc(tail_done, 1)
                    wait(dve, xch_done, c + 1)
                    V.tensor_tensor(xcl[:, i, :], xc[:, i, :], xch[:, i, :].bitcast(f32), ALU.subtract).then_inc(xcl_done, 1)
                for i in range(2):
                    skip(NB)
                    for k in range(2 * NB):
                        jobs[i] = plan.take(last=k == 2 * NB - 1)

            def lru_back(g, adds):
                for i in range(2):
                    c = 2 * g + i
                    wait(dve, free[jobs[i].bank], jobs[i].after)
                    stt(ti[:, i, :], ti[:, i, :], 1.0, xc[:, i, :], ALU.add, ALU.mult).then_inc(ix_done, 1)
                adds(0)
                for i in range(2):
                    c = 2 * g + i
                    wait(dve, aa_done, c + 1)
                    stt(xc[:, i, :], xc[:, i, :], 1.0, xp[:, i, 0:T], ALU.add, ALU.mult).then_inc(msq_done, 1)
                    adds(1 + i)
                adds(3)
                for i in range(2):
                    c = 2 * g + i
                    wait(dve, mult_done, c + 1)
                    V.memset(xc[:, i, 0:1], 1.0).then_inc(one_done, 1)
                    wait(dve, one_done, c + 1)
                    stt(ti[:, i, :], xc[:, i, :], 0.5, ti[:, i, :], ALU.mult, ALU.mult).then_inc(b_done, 1)
                    wait(dve, b_done, c + 1)
                    V.tensor_tensor_scan(xc[:, i, 0:SEQ], aa[:, i, 0:SEQ], ti[:, i, 0:SEQ], 0.0, ALU.mult, ALU.add)\
                        .then_inc(h_done, 1)
                    V.tensor_tensor_scan(xc[:, i, SEQ:T], aa[:, i, SEQ:T], ti[:, i, SEQ:T], vg[:, i, V_H0:V_H0 + 1],
                                         ALU.mult, ALU.add).then_inc(h_done, 1)
                    if i == 0:
                        adds(4)
                    wait(dve, h_done, 2 * c + 2)
                    if i == 1:
                        adds(7)
                    V.tensor_copy(tail[:, c, 6:8], xc[:, i, SEQ - 1:T:DEC]).then_inc(tail_done, 1)
                    V.tensor_tensor(gel[:, i, :], gel[:, i, :], xc[:, i, :], ALU.mult).then_inc(prod_done, 1)
                    if i == 0:
                        adds(5)
                        adds(6)
                for i in range(2):
                    wait(dve, ph_done, 2 * g + i + 1)
                    V.tensor_tensor(pl[:, i, :], gel[:, i, :], ph[:, i, :].bitcast(f32), ALU.subtract).then_inc(pl_done, 1)

            jobs = [None, None]
            lru_front(0, True)
            lru_back(0, lambda m: None)
            dve.wait_ge(lru_zero_done, 2)
            with dve.Fori(1, GROUPS) as g:
                plan.loop(g, 1, JOBS_L, L_FRONT + 2)
                lru_front(g, False)
                lru_back(g, lambda m: add_down(m // 4, [m % 4]))
            plan.end(GROUPS - 1)

            for t in range(9):
                if t == 8:
                    plan.units.add()
                plan.take(last=t == 8)
            add_down(0)
            add_down(1)

            def rope(base, k):
                x = blk(k % NB)
                wait(dve, rot_done, base + k + 1)
                wait(dve, rope_done, base + k)
                V.tensor_tensor(rt2[:, :], aux1[:, 0:BW], cs[:, 1, x], ALU.mult).then_inc(rot_used, 1)
                V.tensor_tensor(rt1[:, :], qsb[:, k % 2, :], cs[:, 0, x], ALU.mult).then_inc(t1_done, 1)
                wait(dve, rot_used, base + k + 1)
                wait(dve, t1_done, base + k + 1)
                V.tensor_tensor(rt1[:, :], rt1[:, :], rt2[:, :], ALU.add).then_inc(rsum_done, 1)
                wait(dve, std_done, base + k + 1)
                V.reciprocal(qstd[:, k % 2, :], qstd[:, k % 2, :]).then_inc(rrec_done, 1)
                wait(dve, rsum_done, base + k + 1)
                wait(dve, rrec_done, base + k + 1)

            def rope_k(k):
                rope(0, k)
                if k >= 2:
                    dve.wait_ge(k_stored[k % 2], 16 * {2: 1, 3: 1, 4: 5, 5: 2}[k])
                V.tensor_tensor(kst[:, k % 2, :], rt1[:, :], qstd[:, k % 2, :], ALU.mult).then_inc(rope_done, 1)

            def rope_q(base, k):
                rope(base, k)
                n = k % NB
                dst = qt[:, 2 * n * BW:2 * (n + 1) * BW].rearrange("p (b i t) -> p b i t", i=2, t=HT)
                V.tensor_tensor(dst[:, :, k // NB, :], rt1[:, :].rearrange("p (b t) -> p b t", t=HT),
                                qstd[:, k % 2, :].rearrange("p (b t) -> p b t", t=HT), ALU.mult).then_inc(rope_done, 1)

            dve.wait_ge(cs_loaded, 16)
            V.memset(kg[HD:P, 0, :], 0.0).then_inc(kz_done, 1)
            V.memset(kg[0:HD, 1, :], 0.0).then_inc(kz_done, 1)
            skip(4 * NB)
            for k in range(6):
                rope_k(k)
            for k in range(5):
                rope_q(6, k)

            def gated(m, n):
                job = plan.take(last=n == NB - 1)
                dve.wait_ge(free[job.bank], job.after)
                stt(acc[:, m, blk(n)], tg[:, n, :], 1.0, acc[:, m, blk(n)], ALU.add, ALU.mult).then_inc(gb_done, 1)

            for m in range(KC - 2):
                for n in range(NB):
                    gated(m, n)
                if m == 0:
                    rope_q(6, 5)

            def attention_step(g, i):
                n0 = g * AU
                new, old = i < AU, 0 <= i - 1 < AU
                if old:
                    q1, k1, _ = unit_shape(i - 1)
                    r1, rows1 = (i - 1) % 3, slice(0, 2 * q1)
                    wait(dve, exp_done, n0 + i)
                    V.tensor_tensor(sm[rows1, r1, 5, :], sm[rows1, r1, 3, :], sm[rows1, r1, 4, :], ALU.add)\
                        .then_inc(den_done, 1)
                if new:
                    q, k, _ = unit_shape(i)
                    r, rows = i % 3, slice(0, 2 * q)
                    wait(dve, s_done, n0 + i + 1)
                    V.tensor_reduce(sm[rows, r, 0, :], sbank[i % 2][rows, 0:256].rearrange("p (h k) -> p h k", h=2)[:, :, 0:k],
                                    AX.X, ALU.max).then_inc(mx_done, 1)
                if old:
                    wait(dve, den_done, n0 + i)
                    V.reciprocal(sm[rows1, r1, 5, :], sm[rows1, r1, 5, :]).then_inc(rc_done, 1)
                if new:
                    wait(dve, mx_done, n0 + i + 1)
                    stt(sm[rows, r, 1, :], sm[rows, r, 0, :], -HD ** -0.5, snk[rows, 0, :], ALU.mult, ALU.min)\
                        .then_inc(nm0_done, 1)
                if old:
                    wait(dve, rc_done, n0 + i)
                    V.tensor_tensor(pr[rows1, r1, :, 0:k1], pr[rows1, r1, :, 0:k1],
                                    sm[rows1, r1, 5, :].rearrange("p (h k) -> p h k", k=1).to_broadcast([2 * q1, 2, k1]),
                                    ALU.mult).then_inc(p_done, 1)
                if new:
                    wait(dve, nm0_done, n0 + i + 1)
                    V.tensor_tensor(sm[rows, r, 2, :], sm[rows, r, 1, :], snk[rows, 1, :], ALU.add).then_inc(nm_done, 1)
                if 0 <= i - 3 < AU:
                    q, _, _ = unit_shape(i - 3)
                    wait(dve, o_done, n0 + i - 2)
                    if i >= 5:
                        wait(dve, oh_done, n0 + i - 4)
                        wait(dve, ol_done, n0 + i - 4)
                    V.tensor_copy(o32[:, (i + 1) % 2, :, 0:q].rearrange("p i (b t) -> p b i t", t=HT),
                                  aux0[:, 0:2 * q].rearrange("p (b i t) -> p b i t", i=2, t=HT)).then_inc(o32_done, 1)
                if 0 <= i - 4 < AU:
                    q, _, q0 = unit_shape(i - 4)
                    wait(dve, oh_done, n0 + i - 3)
                    V.tensor_tensor(ol[:, :, q0:q0 + q], o32[:, i % 2, :, 0:q], oh[:, :, q0:q0 + q].bitcast(f32),
                                    ALU.subtract).then_inc(ol_done, 1)

            def group(g, first, last):
                if not first:
                    rope_q(6 * g + 6, 5)
                V.tensor_copy(snk[:, 0, :], nsink[:, bass.ds(2 * g, 2)]).then_inc(snk_done, 1)
                V.tensor_copy(snk[:, 1, :], sink[:, bass.ds(2 * g, 2)]).then_inc(snk_done, 1)
                wait(dve, snk_done, 2 * g + 2)
                if not first:
                    skip(NB)

                def side_job(j):
                    if first:
                        gated(KC - 2 + j // NB, j % NB)
                    else:
                        add_down_block(j)

                def side_end(j):
                    return 3 * KC * (j + 1) if first else 3 * KC * NB + 6 * (j + 1)

                j = 0
                for i in range(ASLOTS + 2):
                    while j < (2 * NB if first else KC * NB) and (i >= ASLOTS or side_end(j) <= step_mm(i)):
                        side_job(j)
                        j += 1
                    attention_step(g, i)
                skip(2 * NB if first else NB)
                if first:
                    for half in range(2):
                        dve.wait_ge(mb_stored[half], 16 * 4)
                        V.memset(acc[:, 4 * half:4 * half + 4, :], 0.0).then_inc(zero_done, 1)
                    dve.wait_ge(zero_done, 2)
                if not last:
                    skip(2 * NB)
                    for k in range(5):
                        rope_q(6 * g + 12, k)

            def add_down_block(k):
                job = side_down(plan, k)
                wait(dve, *job.done)
                a = acc[:, k % KC, blk(k // KC)]
                V.tensor_tensor(a, bank[job.bank][:, 0:BW], a, ALU.add).then_inc(free[job.bank], 1)

            plan.ring(RING_A)
            group(0, True, False)
            with dve.Fori(1, GROUPS - 1) as g:
                plan.loop(g, 1, JOBS_A, 6)
                group(g, False, False)
            plan.end(GROUPS - 2)
            group(GROUPS - 1, False, True)
            plan.ring(6)

            for m in range(KC):
                job = add_down(m // 4, [m % 4])
                if m == 2:
                    V.memset(ssum[:, :], 0.0).then_inc(zero_done, 1)
                dve.wait_ge(free[job.bank], job.after)
                dve.wait_ge(mg_loaded[m % 5], 32 * (m // 5 + 1))
                stt(mg[:, m % 5, 0, :], mg[:, m % 5, 0, :], 1.0, acc[:, m, :], ALU.add, ALU.mult).then_inc(mg1_done, 1)
                dve.wait_ge(mg1_done, m + 1)
                V.tensor_tensor(mg[:, m % 5, 0, :], mg[:, m % 5, 0, :], mg[:, m % 5, 1, :], ALU.add).then_inc(mg2_done, 1)
            dve.wait_ge(zero_done, 3)

            def x1_low(m, n, s):
                wait(dve, n2h_done, NB * m + n + 1)
                stt(n2l[:, m, blk(n)], acc[:, m, blk(n)], vt[:, m, V_G2:V_G2 + 1], n2h[:, m, blk(n)].bitcast(f32),
                    ALU.mult, ALU.subtract).then_inc(n2l_done, 1)
                wait(dve, x1sq_done, NB * m + n + 1)
                V.tensor_tensor(ssum[:, blk(n)], ssum[:, blk(n)], x1sq[:, (s + n) % 2, :], ALU.add).then_inc(ssum_done, 1)

            with dve.Fori(0, KC // 2) as i:
                plan.loop(i, 0, 2 * NB, 2)
                for s in range(2):
                    m = 2 * i + s
                    for n in range(NB):
                        job = plan.take(last=n == NB - 1)
                        wait(dve, *job.done)
                        wait(dve, xr_loaded[n], 16 * m + 16)
                        stt(acc[:, m, blk(n)], bank[job.bank][:, 0:BW], 0.5, xr[:, n, :], ALU.mult, ALU.add)\
                            .then_inc(free[job.bank], 1)
                        if n >= 1:
                            x1_low(m, n - 1, s)
                    x1_low(m, NB - 1, s)
            plan.end(KC // 2)
            for n in range(NB):
                dve.wait_ge(std2_done, n + 1)
                V.reciprocal(ssum[:, blk(n)], ssum[:, blk(n)]).then_inc(rstd2_done, 1)

            def ffn_front(i, slot):
                for c in range(2):
                    b0 = 6 * i + NB * c
                    for n in range(NB):
                        job = plan.take(last=n == NB - 1)
                        wait(dve, *job.done)
                        wait(dve, h32_done, b0 + n - 2)
                        wait(dve, rstd2_done, n + 1)
                        V.tensor_tensor(sg[:, n, :], bank[job.bank][:, 0:BW], ssum[:, blk(n)], ALU.mult)\
                            .then_inc(free[job.bank], 1)

                    def low(n):
                        wait(dve, hh_done, b0 + n + 1)
                        V.tensor_tensor(hl[:, slot, c, blk(n)], tu[:, (c + n) % 2, :],
                                        hh[:, slot, c, blk(n)].bitcast(f32), ALU.subtract).then_inc(hl_done, 1)

                    for n in range(NB):
                        job = plan.take(last=n == NB - 1)
                        b = (c + n) % 2
                        wait(dve, *job.done)
                        wait(dve, hl_done, b0 + n - 1)
                        V.tensor_tensor(tu[:, b, :], bank[job.bank][:, 0:BW], ssum[:, blk(n)], ALU.mult)\
                            .then_inc(free[job.bank], 1)
                        wait(dve, free[job.bank], job.after)
                        wait(dve, silu_done, b0 + n + 1)
                        V.tensor_tensor(tu[:, b, :], tu[:, b, :], sg[:, n, :], ALU.mult).then_inc(h32_done, 1)
                        if n >= 1:
                            low(n - 1)
                    low(NB - 1)

            ffn_front(0, 0)
            with dve.Fori(0, FFI // 2) as j:
                plan.loop(j, 0, JOBS_F, 12)
                for s in range(2):
                    ffn_front(2 * j + 1 + s, 1 - s)
                    add_down(0)
                    add_down(1)
            plan.end(FFI // 2)
            for m in range(KC):
                first_bank = plan.bank
                add_down(m // 4, [m % 4])
                final_jobs.append([(b, plan.uses[b].value()) for b in range(first_bank, first_bank + NB)])

        @block.sync
        def _(sp):
            sp.dma_start(small[:, :], small_in).then_inc(small_in_s, 16)
            for half in range(2):
                c4 = slice(4 * half, 4 * half + 4)
                sp.dma_start(acc[:, c4, blk(0)], x_in[:, c4, blk(0)]).then_inc((x_in_s[0], x_half_s)[half], 16)
            for u in range(2):
                sp.dma_start(wraw[:, u, :], w_in[u]).then_inc(raw_loaded[u], 16)
            for n in range(1, NB):
                sp.dma_start(acc[:, :, blk(n)], x_in[:, :, blk(n)]).then_inc(x_in_s[n], 16)
            with sp.Fori(1, N_UNITS // 2) as i:
                for u in range(2):
                    wait(sp, split_done, 8 * i + 4 * u - 4)
                    sp.dma_start(wraw[:, u, :], w_in[2 * i + u]).then_inc(raw_loaded[u], 16)
            for m in range(KC):
                for n in range(NB):
                    sp.wait_ge(free[final_jobs[m][n][0]], final_jobs[m][n][1])
                    if m == KC - 1:
                        sp.dma_start(y_out[m, :, blk(n)], acc[:, m, blk(n)]).then_inc(stored, 16)
                if m < KC - 1:
                    sp.dma_start(y_out[m], acc[:, m, :]).then_inc(stored, 16)
            sp.wait_ge(stored, 16 * (KC - 1 + NB + 3))
            for i in range(2):
                sp.wait_ge(k_stored[i], 16 * 6)
                sp.wait_ge(mb_stored[i], 16 * 4)
                sp.wait_ge(v_stored[i], 16 * (5 - i))
            for n in range(NB):
                sp.wait_ge(ta_stored[n], 16 * KC)
            sp.wait_ge(kv_stored, 16 * 3)




def weight_units(w):
    w_in, wao, wlo, wo = w["w_in"][0], w["w_attn_out"][0], w["w_lru_out"][0], w["w_o"][0]
    wgu, wd, wr, wi = w["w_gate_up"][0], w["w_down"][0], w["w_rg"][0], w["w_ig"][0]
    q0, k0, v0, x0, y0, a0 = 0, D, D + KVH * HD, D + 2 * KVH * HD, 2 * D + 2 * KVH * HD, 3 * D + 2 * KVH * HD
    b0 = a0 + D

    def cols(m, c0):
        return m[:, c0:c0 + P].reshape(KC, P, P).transpose(1, 0, 2).reshape(P, UW)

    def rows(m, pair):
        part = m[pair * 2 * P:(pair + 1) * 2 * P].reshape(2, P, 2, 4, P)
        return [part[:, :, h].transpose(1, 2, 0, 3).reshape(P, UW) for h in range(2)]

    def gates(c):
        out = np.zeros((P, UW), w_in.dtype)
        for b in range(2):
            r = slice(b * HD, (b + 1) * HD)
            out[r, b * HD:(b + 1) * HD] = wr[2 * c + b]
            out[r, P + b * HD:P + (b + 1) * HD] = wi[2 * c + b]
        return out

    def front(g):
        return ([cols(w_in, x0 + (2 * g + i) * P) for i in range(2)]
                + [u for i in range(2) for u in (cols(w_in, y0 + (2 * g + i) * P), gates(2 * g + i))])

    def queries(g):
        return [cols(w_in, q0 + (2 * g + i) * P) for i in range(2)]

    def hidden(i):
        return [cols(wgu, h * FF + (2 * i + c) * P) for c in range(2) for h in range(2)]

    units = front(0)
    for g in range(1, GROUPS):
        units += front(g) + rows(wlo, g - 1)
    units += [w_in[h * 512:(h + 1) * 512, v0:v0 + KVH * HD].reshape(4, P, KVH * HD).transpose(1, 0, 2).reshape(P, UW)
              for h in range(2)]
    units += rows(wlo, GROUPS - 1)
    units += [cols(w_in, k0 + i * P) for i in range(2)] + queries(0)
    units += [cols(w_in, b0 + m * P) for m in range(KC)]
    for g in range(GROUPS):
        units += [cols(w_in, a0 + 2 * g * P)] + (rows(wao, g - 1) if g else [])
        units += [cols(w_in, a0 + (2 * g + 1) * P)]
        if g < GROUPS - 1:
            units += queries(g + 1)
    units += rows(wao, GROUPS - 1)
    units += [cols(wo, m * P) for m in range(KC)]
    units += hidden(0)
    for i in range(1, FFI):
        units += hidden(i) + rows(wd, i - 1)
    units += rows(wd, FFI - 1)
    return np.stack(units)


def by_feature(a):
    a = np.moveaxis(a, -1, 0)
    return np.moveaxis(a.reshape((KC, P) + a.shape[1:]), 0, 1)


def rope_tables():
    freqs = np.float32(THETA) ** (-np.arange(0, ROT, 2, dtype=np.float32) / np.float32(ROT))
    pos = np.concatenate([np.arange(SEQ), PAST + np.arange(DEC)]).astype(np.float32)
    ang = freqs[:, None] * pos[None, :]
    cos, sin = np.ones((HD, T), np.float32), np.zeros((HD, T), np.float32)
    cos[:ROT], sin[:ROT] = np.tile(np.cos(ang), (2, 1)), np.tile(np.sin(ang), (2, 1))
    return np.stack([np.tile(cos, (2, 1)), np.tile(sin, (2, 1))], 1)


def constants():
    blk, perm = np.zeros((P, P), np.float32), np.zeros((P, P), np.float32)
    for h in range(2):
        b = h * HD
        blk[b:b + HD, b:b + HD] = 1
        for d in range(ROT // 2):
            perm[b + ROT // 2 + d, b + d] = -1
            perm[b + d, b + ROT // 2 + d] = 1
    return [np.eye(P, dtype=np.float32), np.ones((P, P), np.float32), blk, perm]


def kernel(**inputs):
    import concourse.bacc as _bacc
    from concourse.bass_utils import run_bass_kernel_spmd as _run

    a = {k: np.asarray(v) for k, v in inputs.items()}
    x = np.concatenate([a["x_prompt"][0], a["x_sample"][0]], 0)
    vectors = np.stack([a["attn_norm"][0], a["ffn_norm"][0], *a["conv_w"][0], a["conv_b"][0], a["b_rg"][0], a["b_ig"][0],
                        a["lru_lambda"][0], *a["state_conv"][0, 0], a["state_lru"][0, 0]])
    sinks = np.tile(np.repeat(a["sinks"][0].reshape(GROUPS, 2, 2).transpose(1, 0, 2).reshape(2, 8), HT, 0), (2, 1))
    gains = np.stack([np.tile(a["q_norm"][0], 2), np.tile(a["k_norm"][0], 2)], 1)
    small = np.concatenate(constants() + [by_feature(vectors).reshape(P, KC * NV_IN), gains, sinks], 1)
    arrays = {
        "small": small,
        "x": np.ascontiguousarray(by_feature(x)),
        "rope": rope_tables(),
        "weights": weight_units(a),
        "cache_k": np.ascontiguousarray(a["cache_k"][0, 0].reshape(WINDOW, KVH * HD).T),
        "cache_v": np.ascontiguousarray(a["cache_v"][0, 0].reshape(WINDOW, KVH * HD)),
    }
    outs = {"y": (KC, P, T), "kp": (KVH * HD, WINDOW), "vp": (WINDOW, KVH * HD), "ks": (KVH * HD, WINDOW),
            "vs": (WINDOW, KVH * HD), "tail": (P, KC, 8)}

    nc = _bacc.Bacc("TRN2", target_bir_lowering=False, num_devices=1)
    args = [nc.dram_tensor(f"in_{k}", v.shape, mybir.dt.float32, kind="ExternalInput").ap() for k, v in arrays.items()]
    args += [nc.dram_tensor(f"out_{k}", s, mybir.dt.float32, kind="ExternalOutput").ap() for k, s in outs.items()]
    build(nc, *args)
    r = _run(nc, [{f"in_{k}": v for k, v in arrays.items()}], core_ids=[0]).results[0]

    y = np.ascontiguousarray(np.asarray(r["out_y"]).reshape(D, T).T)
    cache = (1, 1, WINDOW, KVH, HD)
    keys = [np.ascontiguousarray(np.asarray(r[k]).T).reshape(cache) for k in ("out_kp", "out_ks")]
    tail = np.asarray(r["out_tail"]).transpose(2, 1, 0).reshape(8, D)
    return (y[None, :SEQ], y[None, SEQ:],
            keys[0], np.asarray(r["out_vp"]).reshape(cache), tail[None, None, 0:3], tail[None, 6:7],
            keys[1], np.asarray(r["out_vs"]).reshape(cache), tail[None, None, 3:6], tail[None, 7:8])
```
